# Optimizing a Trainium2 kernel written in Bass

```python
import numpy as np
import jax, jax.numpy as jnp
from jax import lax

D_MODEL = 1024
BATCH = 1
SEQ = 512
DEPTH = 1
DEC_BATCH = 8
DEC_SEQ = 1
PAST_LEN = 256
PAGE_SIZE = 128

HEAD_DIM = 64
H_FOX = 8
H_NSA = 8
H_KV = 2
GQA_GROUP = H_NSA // H_KV
W_FOX = H_FOX * HEAD_DIM
W_NSA = H_NSA * HEAD_DIM
W_KV = H_KV * HEAD_DIM
D_FF = 2816
CMP_STRIDE = 16
CMP_LEN = 32
CMP_RATIO = CMP_LEN // CMP_STRIDE
CMP_HIDDEN = HEAD_DIM
SLC_LEN = 64
SLC_TOPN = 16
WINDOW = 512
ROPE_THETA = 10000.0
Q_BLOCK = 128
EPS = 1e-6
NEG = -1e30
FORCE_SCORE = 1e4
N_PAGES = PAST_LEN // PAGE_SIZE
N_POOL = (5 * DEC_BATCH * N_PAGES + 3) // 4
WIN_BUF = min(WINDOW, PAST_LEN)
IN_SPLITS = (W_FOX, W_FOX, W_FOX, H_FOX, W_NSA, 6 * W_KV, 3 * H_NSA)
IN_COLS = W_FOX * 3 + H_FOX + W_NSA + 6 * W_KV + 3 * H_NSA

kernel_name = 'hymba_fox_nsa_macaron_decode_step'

def rmsnorm(x, g):
    xf = x.astype(jnp.float32)
    y = xf * lax.rsqrt(jnp.mean(xf * xf, axis=-1, keepdims=True) + EPS)
    return (y * g.astype(jnp.float32)).astype(x.dtype)

def swiglu(x, wg, wu, wd):
    return (jax.nn.silu(x @ wg) * (x @ wu)) @ wd

def half_ffn(x, g_pre, wg, wu, wd, g_post):
    return x + 0.5 * rmsnorm(swiglu(rmsnorm(x, g_pre), wg, wu, wd), g_post)

def rope(x, pos):
    half = HEAD_DIM // 2
    inv = ROPE_THETA ** (-jnp.arange(half, dtype=jnp.float32) / half)
    ang = pos.astype(jnp.float32)[:, None] * inv[None, :]
    cos = jnp.cos(ang)[None, :, None, :]
    sin = jnp.sin(ang)[None, :, None, :]
    xf = x.astype(jnp.float32)
    x1, x2 = xf[..., :half], xf[..., half:]
    return jnp.concatenate([x1 * cos - x2 * sin, x2 * cos + x1 * sin], axis=-1).astype(x.dtype)

def blocked_over_queries(fn, *xs):
    n_q = xs[0].shape[1]
    qb = min(Q_BLOCK, n_q)
    nb = -(-n_q // qb)
    pad = nb * qb - n_q

    def split(x):
        x = jnp.pad(x, [(0, 0), (0, pad)] + [(0, 0)] * (x.ndim - 2), mode='edge')
        x = x.reshape(x.shape[0], nb, qb, *x.shape[2:])
        return jnp.moveaxis(x, 1, 0)

    out = lax.map(lambda a: fn(*a), tuple(split(x) for x in xs))
    out = jnp.moveaxis(out, 0, 1)
    out = out.reshape(out.shape[0], nb * qb, *out.shape[3:])
    return out[:, :n_q]

def project(n, w_in, b_f, pos):
    B, T = n.shape[:2]
    cuts, acc = [], 0
    for s in IN_SPLITS[:-1]:
        acc += s
        cuts.append(acc)
    parts = jnp.split(n @ w_in, cuts, axis=-1)
    fq = parts[0].reshape(B, T, H_FOX, HEAD_DIM)
    fk = parts[1].reshape(B, T, H_FOX, HEAD_DIM)
    fv = parts[2].reshape(B, T, H_FOX, HEAD_DIM)
    logf = jax.nn.log_sigmoid(parts[3].astype(jnp.float32) + b_f.astype(jnp.float32))
    nq = rope(parts[4].reshape(B, T, H_NSA, HEAD_DIM), pos)
    kvraw = parts[5].reshape(B, T, 3, 2, H_KV, HEAD_DIM)
    ks = rope(kvraw[:, :, :, 0].reshape(B, T, 3 * H_KV, HEAD_DIM), pos).reshape(B, T, 3, H_KV, HEAD_DIM)
    nkv = jnp.stack([ks, kvraw[:, :, :, 1]], axis=3).reshape(B, T, 6, H_KV, HEAD_DIM)
    ng = jax.nn.sigmoid(parts[6].reshape(B, T, H_NSA, 3))
    return fq, fk, fv, logf, nq, nkv, ng

def fox_attention(q, k, v, cum, qpos):
    L = k.shape[1]
    kpos = jnp.arange(L, dtype=jnp.int32)
    cum_t = jnp.swapaxes(cum, 1, 2)
    scale = HEAD_DIM ** -0.5

    def blk(qb_, pb):
        p = pb[0]
        s = jnp.einsum('bqhd,bkhd->bhqk', qb_, k, preferred_element_type=jnp.float32) * scale
        s = s + jnp.take(cum_t, p, axis=2)[..., None] - cum_t[:, :, None, :]
        s = jnp.where(kpos[None, None, None, :] <= p[None, None, :, None], s, NEG)
        a = jax.nn.softmax(s, axis=-1).astype(v.dtype)
        return jnp.einsum('bhqk,bkhd->bqhd', a, v)

    return blocked_over_queries(blk, q, qpos[None, :])

def compress(x, w1, w2, pe):
    B, L = x.shape[:2]
    n_ch = L // CMP_STRIDE
    n_cmp = n_ch - CMP_RATIO + 1
    seg = CMP_STRIDE * HEAD_DIM
    ch = x[:, :n_ch * CMP_STRIDE].reshape(B, n_ch, CMP_STRIDE, H_KV, HEAD_DIM)
    ch = jnp.swapaxes(ch, 2, 3).reshape(B, n_ch, H_KV, seg)
    hid = pe.reshape(-1) @ w1
    for r in range(CMP_RATIO):
        hid = hid + ch[:, r:r + n_cmp] @ w1[r * seg:(r + 1) * seg]
    return jax.nn.gelu(hid) @ w2

def nsa_attention(q, g, kv, kw, pw0, qpos, wk1, wk2, pek, wv1, wv2, pev):
    B, L = kv.shape[:2]
    dtype = kv.dtype
    scale = HEAD_DIM ** -0.5
    kc = compress(kv[:, :, 0], wk1, wk2, pek)
    vc = compress(kv[:, :, 1], wv1, wv2, pev)
    n_cmp = kc.shape[1]
    cmp_start_np = np.arange(n_cmp) * CMP_STRIDE
    cmp_end_np = cmp_start_np + CMP_LEN - 1
    n_slc = -(-L // SLC_LEN)
    slc_start_np = np.arange(n_slc) * SLC_LEN
    overlap = jnp.asarray(((cmp_start_np[None, :] <= (slc_start_np + SLC_LEN - 1)[:, None])
                           & (cmp_end_np[None, :] >= slc_start_np[:, None])).astype(np.float32))
    cmp_end = jnp.asarray(cmp_end_np.astype(np.int32))
    slc_start = jnp.asarray(slc_start_np.astype(np.int32))
    pad = n_slc * SLC_LEN - L

    def to_blocks(x):
        x = jnp.pad(x, ((0, 0), (0, pad), (0, 0), (0, 0)))
        return x.reshape(B, n_slc, SLC_LEN, H_KV, HEAD_DIM).transpose(0, 3, 1, 2, 4)

    kb = to_blocks(kv[:, :, 2])
    vb = to_blocks(kv[:, :, 3])
    n_sel = min(SLC_TOPN, n_slc)
    Lw = kw.shape[1]
    gather = jax.vmap(jax.vmap(lambda blocks, ids: blocks[ids]))
    blk_ids = jnp.arange(n_slc, dtype=jnp.int32)
    in_blk = jnp.arange(SLC_LEN, dtype=jnp.int32)

    def blk(qb_, gb, pb):
        p = pb[0]
        nq = p.shape[0]
        qg = qb_.reshape(B, nq, H_KV, GQA_GROUP, HEAD_DIM)
        s = jnp.einsum('bqhgd,bnhd->bhgqn', qg, kc, preferred_element_type=jnp.float32) * scale
        ok = cmp_end[None, :] <= p[:, None]
        a_cmp = jnp.where(ok, jax.nn.softmax(jnp.where(ok, s, NEG), axis=-1), 0.0)
        o_cmp = jnp.einsum('bhgqn,bnhd->bqhgd', a_cmp.astype(dtype), vc)
        imp = jnp.einsum('bhgqn,jn->bhqj', a_cmp, overlap)
        qblk = p // SLC_LEN
        forced = (blk_ids[None, :] == 0) | (blk_ids[None, :] == qblk[:, None]) | (blk_ids[None, :] == qblk[:, None] - 1)
        valid = slc_start[None, :] <= p[:, None]
        score = jnp.where(valid, jnp.where(forced, FORCE_SCORE, imp), -1.0)
        _, idx = lax.top_k(score, n_sel)
        ksel = gather(kb, idx)
        vsel = gather(vb, idx)
        tpos = idx[..., None] * SLC_LEN + in_blk
        s = jnp.einsum('bqhgd,bhqnld->bhgqnl', qg, ksel, preferred_element_type=jnp.float32) * scale
        s = jnp.where((tpos <= p[:, None, None])[:, :, None], s, NEG)
        a = jax.nn.softmax(s.reshape(B, H_KV, GQA_GROUP, nq, n_sel * SLC_LEN), axis=-1)
        a = a.reshape(B, H_KV, GQA_GROUP, nq, n_sel, SLC_LEN).astype(dtype)
        o_slc = jnp.einsum('bhgqnl,bhqnld->bqhgd', a, vsel)
        sw = min(Lw, WINDOW - 1 + nq)
        start = jnp.clip(p[0] - (WINDOW - 1) - pw0, 0, Lw - sw)
        kwin = lax.dynamic_slice_in_dim(kw, start, sw, axis=1)
        wpos = pw0 + start + jnp.arange(sw, dtype=jnp.int32)
        s = jnp.einsum('bqhgd,bkhd->bhgqk', qg, kwin[:, :, 0], preferred_element_type=jnp.float32) * scale
        dist = p[:, None] - wpos[None, :]
        s = jnp.where((dist >= 0) & (dist < WINDOW), s, NEG)
        a = jax.nn.softmax(s, axis=-1).astype(dtype)
        o_win = jnp.einsum('bhgqk,bkhd->bqhgd', a, kwin[:, :, 1])
        o = jnp.stack([o_cmp, o_slc, o_win], axis=-1).reshape(B, nq, H_NSA, HEAD_DIM, 3)
        return jnp.einsum('bqhdc,bqhc->bqhd', o, gb.astype(o.dtype))

    return blocked_over_queries(blk, q, g, qpos[None, :])

def merge_groups(o_fox, o_nsa, g_fox, g_nsa, w_out):
    B, T = o_fox.shape[:2]
    of = rmsnorm(o_fox.reshape(B, T, W_FOX), g_fox)
    on = rmsnorm(o_nsa.reshape(B, T, W_NSA), g_nsa)
    return jnp.concatenate([of, on], axis=-1) @ w_out

def setup_inputs(seed: int = 0) -> dict:
    key = jax.random.key(seed)
    ks = iter(jax.random.split(key, 40))
    f32 = jnp.float32

    def nrm(shape, scale):
        return scale * jax.random.normal(next(ks), shape, f32)

    def gain(n):
        return 1.0 + nrm((DEPTH, n), 0.05)

    return {
        'x_prompt': nrm((BATCH, SEQ, D_MODEL), 1.0),
        'x_sample': nrm((DEC_BATCH, DEC_SEQ, D_MODEL), 1.0),
        'cache_fox_kv': nrm((DEPTH, N_POOL, PAGE_SIZE, 2, H_FOX, HEAD_DIM), 1.0),
        'cache_fox_logf': jax.nn.log_sigmoid(2.0 + nrm((DEPTH, N_POOL, PAGE_SIZE, H_FOX), 1.0)),
        'cache_nsa_kv': nrm((DEPTH, N_POOL, PAGE_SIZE, 4, H_KV, HEAD_DIM), 1.0),
        'state_nsa_win_kv': nrm((DEPTH, DEC_BATCH, WIN_BUF, 2, H_KV, HEAD_DIM), 1.0),
        'page_table': jax.random.permutation(next(ks), N_POOL)[:DEC_BATCH * N_PAGES].reshape(DEC_BATCH, N_PAGES).astype(jnp.int32),
        'g_ffn1_pre': gain(D_MODEL),
        'w_ffn1_gate': nrm((DEPTH, D_MODEL, D_FF), D_MODEL ** -0.5),
        'w_ffn1_up': nrm((DEPTH, D_MODEL, D_FF), D_MODEL ** -0.5),
        'w_ffn1_down': nrm((DEPTH, D_FF, D_MODEL), D_FF ** -0.5),
        'g_ffn1_post': gain(D_MODEL),
        'g_mix_pre': gain(D_MODEL),
        'w_in': nrm((DEPTH, D_MODEL, IN_COLS), D_MODEL ** -0.5),
        'b_fox_f': 2.0 + nrm((DEPTH, H_FOX), 0.1),
        'w_cmpk_1': nrm((DEPTH, CMP_LEN * HEAD_DIM, CMP_HIDDEN), (CMP_LEN * HEAD_DIM) ** -0.5),
        'w_cmpk_2': nrm((DEPTH, CMP_HIDDEN, HEAD_DIM), CMP_HIDDEN ** -0.5),
        'pe_cmpk': nrm((DEPTH, CMP_LEN, HEAD_DIM), 0.1),
        'w_cmpv_1': nrm((DEPTH, CMP_LEN * HEAD_DIM, CMP_HIDDEN), (CMP_LEN * HEAD_DIM) ** -0.5),
        'w_cmpv_2': nrm((DEPTH, CMP_HIDDEN, HEAD_DIM), CMP_HIDDEN ** -0.5),
        'pe_cmpv': nrm((DEPTH, CMP_LEN, HEAD_DIM), 0.1),
        'g_fox_out': gain(W_FOX),
        'g_nsa_out': gain(W_NSA),
        'w_out': nrm((DEPTH, W_FOX + W_NSA, D_MODEL), (W_FOX + W_NSA) ** -0.5),
        'g_mix_post': gain(D_MODEL),
        'g_ffn2_pre': gain(D_MODEL),
        'w_ffn2_gate': nrm((DEPTH, D_MODEL, D_FF), D_MODEL ** -0.5),
        'w_ffn2_up': nrm((DEPTH, D_MODEL, D_FF), D_MODEL ** -0.5),
        'w_ffn2_down': nrm((DEPTH, D_FF, D_MODEL), D_FF ** -0.5),
        'g_ffn2_post': gain(D_MODEL),
    }

def reference(x_prompt, x_sample, cache_fox_kv, cache_fox_logf, cache_nsa_kv, state_nsa_win_kv, page_table,
              g_ffn1_pre, w_ffn1_gate, w_ffn1_up, w_ffn1_down, g_ffn1_post, g_mix_pre, w_in, b_fox_f,
              w_cmpk_1, w_cmpk_2, pe_cmpk, w_cmpv_1, w_cmpv_2, pe_cmpv, g_fox_out, g_nsa_out, w_out,
              g_mix_post, g_ffn2_pre, w_ffn2_gate, w_ffn2_up, w_ffn2_down, g_ffn2_post):
    f32 = jnp.float32
    pos_p = jnp.arange(SEQ, dtype=jnp.int32)
    pos_s = PAST_LEN + jnp.arange(DEC_SEQ, dtype=jnp.int32)
    win_p_keep = min(WINDOW, SEQ)
    win_s_keep = min(WINDOW, PAST_LEN + DEC_SEQ)
    yp, ys = x_prompt, x_sample
    fkv_p, flf_p, nkv_p, win_p = [], [], [], []
    fkv_s, flf_s, nkv_s, win_s = [], [], [], []
    for l in range(DEPTH):
        ffn1 = (g_ffn1_pre[l], w_ffn1_gate[l], w_ffn1_up[l], w_ffn1_down[l], g_ffn1_post[l])
        ffn2 = (g_ffn2_pre[l], w_ffn2_gate[l], w_ffn2_up[l], w_ffn2_down[l], g_ffn2_post[l])
        cmp_w = (w_cmpk_1[l], w_cmpk_2[l], pe_cmpk[l], w_cmpv_1[l], w_cmpv_2[l], pe_cmpv[l])

        hp = half_ffn(yp, *ffn1)
        fq, fk, fv, logf, nq, nkv, ng = project(rmsnorm(hp, g_mix_pre[l]), w_in[l], b_fox_f[l], pos_p)
        o_fox = fox_attention(fq, fk, fv, jnp.cumsum(logf, axis=1), pos_p)
        o_nsa = nsa_attention(nq, ng, nkv[:, :, :4], nkv[:, :, 4:], 0, pos_p, *cmp_w)
        hp = hp + rmsnorm(merge_groups(o_fox, o_nsa, g_fox_out[l], g_nsa_out[l], w_out[l]), g_mix_post[l])
        yp = half_ffn(hp, *ffn2)
        fkv_p.append(jnp.stack([fk, fv], axis=2))
        flf_p.append(logf)
        nkv_p.append(nkv[:, :, :4])
        win_p.append(nkv[:, SEQ - win_p_keep:, 4:])

        hs = half_ffn(ys, *ffn1)
        fq, fk, fv, logf, nq, nkv, ng = project(rmsnorm(hs, g_mix_pre[l]), w_in[l], b_fox_f[l], pos_s)
        past_fkv = cache_fox_kv[l][page_table].reshape(DEC_BATCH, PAST_LEN, 2, H_FOX, HEAD_DIM)
        past_lf = cache_fox_logf[l][page_table].reshape(DEC_BATCH, PAST_LEN, H_FOX)
        k_all = jnp.concatenate([past_fkv[:, :, 0], fk], axis=1)
        v_all = jnp.concatenate([past_fkv[:, :, 1], fv], axis=1)
        cum = jnp.cumsum(jnp.concatenate([past_lf.astype(f32), logf], axis=1), axis=1)
        o_fox = fox_attention(fq, k_all, v_all, cum, pos_s)
        past_nkv = cache_nsa_kv[l][page_table].reshape(DEC_BATCH, PAST_LEN, 4, H_KV, HEAD_DIM)
        kv_all = jnp.concatenate([past_nkv, nkv[:, :, :4]], axis=1)
        kw_all = jnp.concatenate([state_nsa_win_kv[l], nkv[:, :, 4:]], axis=1)
        o_nsa = nsa_attention(nq, ng, kv_all, kw_all, PAST_LEN - state_nsa_win_kv.shape[2], pos_s, *cmp_w)
        hs = hs + rmsnorm(merge_groups(o_fox, o_nsa, g_fox_out[l], g_nsa_out[l], w_out[l]), g_mix_post[l])
        ys = half_ffn(hs, *ffn2)
        fkv_s.append(jnp.stack([fk, fv], axis=2))
        flf_s.append(logf)
        nkv_s.append(nkv[:, :, :4])
        win_s.append(kw_all[:, kw_all.shape[1] - win_s_keep:])

    new_fox_kv_prompt = jnp.stack(fkv_p, axis=0)
    new_fox_logf_prompt = jnp.stack(flf_p, axis=0)
    new_nsa_kv_prompt = jnp.stack(nkv_p, axis=0)
    new_win_kv_prompt = jnp.stack(win_p, axis=0)
    new_fox_kv_sample = jnp.stack(fkv_s, axis=0)
    new_fox_logf_sample = jnp.stack(flf_s, axis=0)
    new_nsa_kv_sample = jnp.stack(nkv_s, axis=0)
    new_win_kv_sample = jnp.stack(win_s, axis=0)
    return (yp, ys, new_fox_kv_prompt, new_fox_logf_prompt, new_nsa_kv_prompt, new_win_kv_prompt,
            new_fox_kv_sample, new_fox_logf_sample, new_nsa_kv_sample, new_win_kv_sample)


_drawn_inputs = setup_inputs


def setup_inputs(seed=0):
    import zlib

    import numpy as np

    out = dict(_drawn_inputs(seed))
    spreads = {}
    factors = {'pe_cmpk': 6.755, 'g_ffn2_post': 3.722}
    for name, (base, spread) in spreads.items():
        noise = np.random.default_rng([zlib.crc32(name.encode()), seed]).standard_normal(out[name].shape)
        drawn = base * np.exp(spread * noise) if base else spread * noise
        out[name] = __import__('jax').numpy.asarray(drawn.astype(out[name].dtype))
    for name, factor in factors.items():
        out[name] = (out[name] * factor).astype(out[name].dtype)
    return out
```

```python
from contextlib import ExitStack

import numpy as np

import concourse.bass as bass
from concourse import mybir

F32 = mybir.dt.float32
F32R = mybir.dt.float32r
BF16 = mybir.dt.bfloat16
I32 = mybir.dt.int32
ALU = mybir.AluOpType
ACT = mybir.ActivationFunctionType
AX = mybir.AxisListType

P = 128
D_MODEL, SEQ, DEC, PAST, PAGE = 1024, 512, 8, 256, 128
TOK = SEQ + DEC
HALF = TOK // 2
DH, HF, HN, HKV = 64, 8, 8, 2
D_FF = 2816
CMP_STRIDE, CMP_LEN = 16, 32
THETA, EPS, NEG = 10000.0, 1e-6, -1e30
KT = D_MODEL // P
FT = D_FF // P
QT = SEQ // P
SCALE = DH ** -0.5
GROUPS = (12, 10)
NPG = PAST // PAGE
NPAGE = DEC * NPG
N_POOL = (5 * NPAGE + 3) // 4
NEWK = PAST + 1
N_CMP = (SEQ - CMP_LEN) // CMP_STRIDE + 1
N_CMP_S = (PAST - CMP_LEN) // CMP_STRIDE + 1
XLEN = SEQ + DEC * PAST + CMP_LEN
N_WIN = (XLEN - CMP_LEN) // CMP_STRIDE + 1
KCMP = NEWK + N_CMP_S
ROWS = DEC * HF
WARM = (34, 28, 20)
HSQ_PE, HSS_AT = 4, 2
DVE_SCALES = 2
KF_SLOTS = 5
HID_FROM, HID_PER_UNIT = 52, 2

TILES = (["fg"] + ["fq"] * 4 + ["fk"] * 4 + ["fv"] * 4
         + ["nq"] * 4 + ["cmpk", "slck", "wink", "cmpv", "slcv", "winv"])
NB1 = 13
NPROJ = len(TILES)
ROPED = ("nq", "cmpk", "slck", "wink")
AUXED = ROPED + ("fg", "fv", "slcv", "winv")
STACKED = ("fq", "nq", "fk", "slck", "wink")
STORED = {5 + n: ("fox", n) for n in range(8)}
STORED.update({17: ("nsa", 0), 20: ("nsa", 1), 18: ("nsa", 2), 21: ("nsa", 3), 19: ("win", 0), 22: ("win", 1)})

CONSTS = [("ident", P), ("ones", P), ("rot", P), ("cos", TOK), ("sin", TOK), ("cmask", P), ("cok", P),
          ("pick", 4 * ROWS), ("is_h", HF), ("is_b", DEC), ("is_kv", HKV), ("eps", 2),
          ("causal", P), ("sel", HF * P)]
GAINS = ["ffn1_pre", "ffn1_post", "mix_pre", "out", "mix_post", "ffn2_pre", "ffn2_post"]

FFN_ITEMS = 2 * FT + 2 * 2 * KT
IT_PROJ = FFN_ITEMS
IT_OUT = IT_PROJ + NPROJ
IT_F2 = IT_OUT + KT
N_ITEMS = IT_F2 + FFN_ITEMS
FFN_STEPS = FFN_ITEMS // 2


def const_columns():
    at, out = 0, {}
    for name, n in CONSTS:
        out[name] = (at, at + n)
        at += n
    return out, at


def ffn_phases():
    out, n, gates = [], 0, 0
    for g, size in enumerate(GROUPS):
        out.append(("gu", g, size, n, gates))
        out.append(("down", g, KT, n + size, gates + size))
        n += size + KT
        gates += size
    return out


def transfers():
    out, k = [], 0
    for f in (1, 2):
        part = []
        for kind, g, size, _, gates in ffn_phases():
            part += [(f"gu{f}", gates + m, 2) if kind == "gu" else (f"down{f}{g}", m, 2) for m in range(size)]
        if f == 1:
            part += [("in", 2 * m, min(2, NPROJ - 2 * m)) for m in range((NPROJ + 1) // 2)]
            part += [("out", 2 * m, 2) for m in range(KT // 2)]
        for name, idx, n in part:
            out.append((name, idx, k, n))
            k += n
    return out


def of_kind(j, kinds):
    return sum(t in kinds for t in TILES[:j])


def unit(v):
    if v < 4 * HF:
        return True, v // 4, 0, v % 4, v // 4
    w = v - 4 * HF
    return False, w // 8, (w // 4) % 2, w % 4, HF + w // 4


def runs_of_pair(t):
    return range(2 * t, 2 * t + 2) if t < 4 else range(HF + 4 * (t - 4), HF + 4 * (t - 3))


class Step:

    def __init__(self, phase, par, m=None, i=None):
        self.kind, self.g, self.size, before, gates = phase
        self.number, self.i, self.par = m, i, par
        self.m = m if i is None else i * 2 + (2 + par)
        self.M = self.m + before
        self.gate = self.m + gates
        self.offset = before + 2 + par


def run_ffn(eng, body):
    for phase in ffn_phases():
        size = phase[2]
        for m in (0, 1):
            body(Step(phase, m, m=m))
        with eng.Fori(0, (size - 4) // 2) as i:
            for par in (0, 1):
                body(Step(phase, par, i=i))
        for m in (size - 2, size - 1):
            body(Step(phase, m % 2, m=m))


def layer_kernel(nc, I, O):
    with ExitStack() as ctx:
        made = {}

        def sem(name):
            if name not in made:
                made[name] = ctx.enter_context(nc.semaphore(name))
            return made[name]

        signals = {"xhi": (KT, "0aob"), "xlo": (KT, "0aob"), "hsq": (KT, "0ab"), "hacc": (1, "0ab"),
                   "hss": (1, "0ab"), "hss_ln": (1, "0ab"), "rstd": (1, "0ab"),
                   "ysq": (KT, "abc"), "yg": (KT, "abc"), "normed": (KT, "abc"), "mixed": (KT, "abc"),
                   "acc": (KT - 1, "abc"), "yss": (1, "abc"), "yss_ln": (1, "abc"), "yrstd": (1, "abc"),
                   "evac": (2 * FFN_STEPS, (0, 1)), "silu": (FT, (0, 1)), "hid": (FT, (0, 1)),
                   "hid_hi": (FT, (0, 1)), "hid_lo": (FT, (0, 1))}

        def since(name, stage, n):
            each, stages = signals[name]
            return n + each * stages.index(stage)

        base = 16640
        room = nc.sbuf_usable_end // 32 * 32 - base - 512
        ctx.enter_context(nc.sbuf_tensor("reserved", [P, room // 4], F32))

        class Region:

            def __init__(self, start, size):
                self.at, self.end = start, start + size

            def put(self, name, shape, dt):
                here = self.at
                size = int(np.prod(shape[1:])) * (2 if dt == BF16 else 4)
                self.at += -(-size // 32) * 32
                assert self.at <= self.end, (name, self.at, self.end)
                return nc.alloc_sbuf_tensor_at(name, shape, dt, offset=here)

        cc, ncol = const_columns()
        kept = cc["causal"][0]
        tile_b = TOK * 4
        fixed = Region(base, 16384)
        C = fixed.put("consts", [P, kept], F32)
        gains = fixed.put("gains", [P, KT * len(GAINS) + 1], F32)
        R1 = fixed.put("token_rstd", [P, TOK], F32)
        identb = fixed.put("identb", [P, P], BF16)
        causalb = fixed.put("causalb", [P, P], BF16)
        selb = fixed.put("selb", [P, HF * P], BF16)
        cumb = fixed.put("cumb", [P, SEQ], BF16)
        row_max = fixed.put("row_max", [P, 96], F32)
        row_sum = fixed.put("row_sum", [P, 96], F32)
        row_inv = fixed.put("row_inv", [P, 96], F32)
        gates = fixed.put("gates", [P, QT, 24], F32)
        fk_new = fixed.put("fk_new", [P, 4, DEC], F32)
        nk_new = fixed.put("nk_new", [P, 2, DEC], F32)
        fq_new = fixed.put("fq_new", [P, 4, DEC], F32)
        nq_new = fixed.put("nq_new", [P, 4, DEC], F32)
        fg_new = fixed.put("fg_new", [P, DEC], F32)
        pages = fixed.put("pages", [1, NPAGE], I32)

        dense = Region(fixed.end, 3 * KT * tile_b + 8 * 4096)
        H = dense.put("H", [P, KT, TOK], F32)
        xh0 = dense.at
        XH = dense.put("XH", [P, KT, TOK], F32R)
        xl0 = dense.at
        XL = dense.put("XL", [P, KT, TOK], F32R)
        w_at = dense.at
        RAW = dense.put("RAW", [P, 2, 2, KT * P], F32)
        WH = dense.put("WH", [P, 2, KT * P], F32R)
        WL = dense.put("WL", [P, 2, KT * P], F32R)
        a0, asize = dense.end, base + room - dense.end

        ffn = Region(a0, asize)
        UH = ffn.put("UH", [P, GROUPS[0], TOK], F32R)
        UL = ffn.put("UL", [P, GROUPS[0], TOK], F32R)
        Y = ffn.put("Y", [P, KT, TOK], F32)
        GT = ffn.put("GT", [P, 2, TOK], F32)
        UT = ffn.put("UT", [P, 2, TOK], F32)
        ST = ffn.put("ST", [P, 2, TOK], F32)
        HT = ffn.put("HT", [P, 2, TOK], F32)
        SQ = ffn.put("SQ", [P, 2, TOK], F32)
        ACC = ffn.put("ACC", [P, TOK], F32)

        att = Region(a0, asize)
        OT = att.put("OT", [P, 8, TOK], F32)
        q0 = att.at
        QST = att.put("QST", [P, 8, 2, SEQ], F32R)
        k0 = att.at
        KST = att.put("KST", [P, 8, SEQ], F32R)
        v0 = att.at
        VT = att.put("VT", [P, QT, 512], F32)
        p0 = att.at
        PTS = att.put("PTS", [P, 2, QT, SEQ], F32)
        t0 = att.at
        TR = att.put("TR", [P, 4, TOK], F32)
        r0 = att.at
        PR = att.put("PR", [P, 4, SEQ], F32)
        att.at = r0 + 4 * tile_b
        v_new = att.put("v_new", [DEC, 768], F32)
        HID = [att.put("HIDK", [P, N_WIN], F32), att.put("HIDV", [P, N_WIN], F32)]
        W2 = att.put("W2", [P, 2, P], F32)
        rope = Region(r0, 4 * tile_b)
        RO = rope.put("RO", [P, 2, TOK], F32)
        RC = rope.put("RC", [P, TOK], F32)
        RS = rope.put("RS", [P, TOK], F32)
        fgr = Region(p0, 16384)
        LF = [fgr.put(f"LF{i}", [P, TOK], F32) for i in range(5)]
        cum_hi = fgr.put("cum_hi", [P, SEQ], BF16)
        late = fgr.put("late", [P, P + HF * P], F32)

        W1 = [nc.alloc_sbuf_tensor_at("W1K", [P, CMP_LEN, P], F32, offset=xh0),
              nc.alloc_sbuf_tensor_at("W1V", [P, CMP_LEN, P], F32, offset=xl0)]
        stage = Region(w_at, 8 * 4096)
        X = [stage.put("XK", [P, XLEN], F32), stage.put("XV", [P, XLEN], F32)]
        QBF = stage.put("QBF", [P, 4, DEC * ROWS], F32)
        QBN = stage.put("QBN", [P, DEC * ROWS], F32)
        KF = Region(w_at, 2 * XLEN * 4).put("KF", [P, KF_SLOTS, 4, NEWK], F32)
        cs = Region(k0, 16384)
        SCT = cs.put("SCT", [P, 2, SEQ], F32)
        SCM = cs.put("SCM", [P, QT, HN, 32], F32)
        PC = cs.put("PC", [P, QT, HN, 32], F32)
        PCT = cs.put("PCT", [P, 2, SEQ], F32)
        cv = Region(v0, 8192)
        kc_new = cv.put("kc_new", [P, P], F32)
        vc_new = cv.put("vc_new", [P, P], F32)
        KCS = cv.put("KCS", [P, 2, P], F32R)
        VCZ = cv.put("VCZ", [P, 4, P], F32)
        cmax = cv.put("cmax", [P, QT, HN], F32)
        csum = cv.put("csum", [P, QT, HN], F32)
        cinv = cv.put("cinv", [P, QT, HN], F32)

        VF = [nc.alloc_sbuf_tensor_at("VF0", [P, 8, 512], F32, offset=xh0),
              nc.alloc_sbuf_tensor_at("VF1", [P, 8, 512], F32, offset=xl0)]
        dq = Region(q0, 32768)
        PZ = [None, None, dq.put("PZW", [P, NPG, DEC * ROWS], F32)]
        SC = [None, None, dq.put("SW", [ROWS, NEWK], F32)]
        dk = Region(k0, 16384)
        KW = dk.put("KW", [P, DEC, NEWK], F32)
        PZ[1] = dk.put("PZS", [P, NPG, DEC * ROWS], F32)
        OS = dk.put("OS", [ROWS, 2, DH], F32)
        dp = Region(p0, 16384)
        KD = dp.put("KD", [P, DEC, KCMP], F32)
        PZ[0] = dp.put("PZF", [P, NPG, DEC * ROWS], F32)
        LFS = dp.put("LFS", [ROWS, NEWK], F32)
        CUMS = dp.put("CUMS", [ROWS, NEWK], F32)
        EN = dp.put("EN", [ROWS, HKV, DH], F32)
        VW = nc.alloc_sbuf_tensor_at("VW", [P, NPAGE, P], F32, offset=t0)
        VS = nc.alloc_sbuf_tensor_at("VS", [P, NPAGE, P], F32, offset=r0)
        dv = Region(v0 + 1024, 7168)
        SC[0] = dv.put("SF", [ROWS, NEWK], F32)
        SC[1] = dv.put("SN", [ROWS, KCMP], F32)
        EF = dv.put("EF", [ROWS, HF, DH], F32)
        PN = dv.put("PN", [ROWS, 3, DEC], F32)
        PNT = dv.put("PNT", [DEC, 3, ROWS], F32)
        PCX = dv.put("PCX", [ROWS, DEC, 16], F32)
        PCZ = dv.put("PCZ", [P, ROWS], F32)
        GB = dv.put("GB", [ROWS, 4, DEC], F32)
        picked = dv.put("picked", [ROWS, 4], F32)
        dmax = dv.put("dmax", [ROWS, 4], F32)
        dsum = dv.put("dsum", [ROWS, 4], F32)
        dinv = dv.put("dinv", [ROWS, 4], F32)

        on = Region(t0, 4 * tile_b)
        OR = on.put("OR", [P, 2, TOK], F32)
        OACC = on.put("OACC", [P, 2, TOK], F32)
        osq = Region(r0, 4 * tile_b)
        OSQ = osq.put("OSQ", [P, 3, TOK], F32)

        ps = ctx.enter_context(nc.psum_tensor("ps", [P, 8, 512], F32))

        def const(name):
            a, b = cc[name]
            return C[:, a:b]

        ident, ones = const("ident"), const("ones")
        cos, sin = const("cos"), const("sin")

        def gain(name, t):
            n = KT * GAINS.index(name) + t
            return gains[:, n:n + 1]

        def halves(slot):
            return ps[:, 2 * slot:2 * slot + 2, 0:HALF]

        def two(ap):
            return ap.rearrange("p (a n) -> p a n", a=2)

        def row(t, n):
            if isinstance(n, int):
                return t[:, n, :]
            return t[:, bass.ds(n, 1), :].rearrange("p a n -> p (a n)")

        def view(ap, start, dims):
            return bass.AP(ap.tensor, ap.offset + start, [list(ap.ap[0])] + dims)

        dmas = transfers()
        where = {}
        for d, (_, _, k, n) in enumerate(dmas):
            for j in range(n):
                where[k + j] = (d, j)
        D_F = (0, len(dmas) - FFN_STEPS)
        IT_F = (0, IT_F2)

        def item_width(k):
            if IT_PROJ <= k < IT_F2:
                return KT * P
            M = (k if k < IT_PROJ else k - IT_F2) // 2
            for kind, g, size, before, _ in ffn_phases():
                if before <= M < before + size:
                    return (KT if kind == "gu" else GROUPS[g] // 2) * P

        w_raw = [sem("w_raw0"), sem("w_raw1")]
        w_hi, w_lo = sem("w_hi"), sem("w_lo")
        used = sem("items_used")

        def raw_behind(f, s, e):
            d = D_F[f] + 1 + s.offset
            return d % 2, s.i * 16 + 16 * (d // 2 + 1), e

        def splitter(eng, part):
            def write(k, par, slot, count, j, width):
                if not isinstance(k, int) or k >= 2:
                    eng.wait_ge(used, k - 1)
                if part == "hi":
                    eng.wait_ge(w_raw[slot], count)
                    nc.scalar.copy(WH[:, par, 0:width], RAW[:, slot, j, 0:width]).then_inc(w_hi, 1)
                else:
                    eng.wait_ge(w_hi, k + 1)
                    nc.vector.tensor_tensor(WL[:, par, 0:width], RAW[:, slot, j, 0:width],
                                            WH[:, par, 0:width], ALU.subtract).then_inc(w_lo, 1)

            def item(k):
                if k < N_ITEMS:
                    d, j = where[k]
                    write(k, k % 2, d % 2, 16 * (d // 2 + 1), j, item_width(k))

            def behind(f, s, e):
                if s.number is not None:
                    item(IT_F[f] + 2 * s.M + 2 + e)
                    return
                slot, count, j = raw_behind(f, s, e)
                width = (KT if s.kind == "gu" else GROUPS[s.g] // 2) * P
                write(s.M * 2 + (IT_F[f] + 2 + e), (IT_F[f] + e) % 2, slot, count, j, width)

            return item, behind

        def stored_sem(j):
            name, n = STORED[j]
            if name == "nsa" and n < 2:
                return f"nsa{n}_stored"
            return f"r_stored{of_kind(j, ROPED) % 2}" if TILES[j] in ROPED else f"t_stored{j % 4}"

        def stored_count(j):
            return 16 * (1 + sum(stored_sem(i) == stored_sem(j) for i in STORED if i < j))

        POST = {"a": "ffn1_post", "b": "mix_post", "c": "ffn2_post"}

        def score_bank(v):
            return v % 4 if unit(v)[0] else (v - 4 * HF) % 3

        def scale_p(eng, tensor_scalar, u):
            fox, h, br, i, _ = unit(u)
            W = P * (i + 1)
            eng.wait_ge(sem("att_inv"), u + 1)
            c = 3 * h + 1 + br
            gate, times = (None, {}) if fox else (gates[:, i, c:c + 1], {"op1": ALU.mult})
            tensor_scalar(PR[:, u % 4, 0:W], PR[:, u % 4, 0:W], row_inv[:, u:u + 1], gate, ALU.mult,
                          **times).then_inc(sem(scaled_by(u)), 1)

        def scaled_by(u):
            return "att_scaled_dve" if unit(u)[3] >= DVE_SCALES else "att_scaled_pool"

        def scaled_count(u):
            return sum(scaled_by(v) == scaled_by(u) for v in range(u + 1))

        def turn_out(eng, copy, w, name):
            _, _, _, i, run = unit(w)
            eng.wait_ge(sem("att_turned"), w + 1)
            if run >= 2:
                eng.wait_ge(sem("att_pv"), run - 1)
            copy(PTS[:, run % 2, 0:i + 1, P * i:P * i + P],
                 ps[:, 4 + w % 2, 0:P * (i + 1)].rearrange("p (a n) -> p a n", n=P)).then_inc(sem(name), 1)

        block = ctx.enter_context(nc.Block())

        @block.sync
        def _(sp):
            def source(name, idx, n):
                if name in ("in", "out"):
                    return I["w_" + name][idx:idx + n].rearrange("i p n -> p i n")
                return I["w_" + name][bass.ds(idx, 1)].rearrange("a p i n -> p (a i) n")

            def stream(first, count):
                for d in range(first, first + count):
                    name, idx, k, n = dmas[d]
                    if d >= 2:
                        done = dmas[d - 2][2] + dmas[d - 2][3]
                        sp.wait_ge(w_hi, done)
                        sp.wait_ge(w_lo, done)
                    width = I["w_" + name].shape[-1]
                    sp.dma_start(RAW[:, d % 2, 0:n, 0:width], source(name, idx, n)).then_inc(w_raw[d % 2], 16)

            def stream_ffn(f, skip):
                for phase in ffn_phases():
                    kind, g, size, before, _ = phase
                    first = D_F[f] + before
                    if not (skip and before == 0):
                        stream(first, 2)
                    name, idx, k, _ = dmas[first + 2]
                    width = I["w_" + name].shape[-1]
                    with sp.Fori(0, (size - 4) // 2) as i:
                        for j in (0, 1):
                            d = first + 2 + j
                            sp.wait_ge(w_hi, i * 4 + (k - 2 + 2 * j))
                            sp.wait_ge(w_lo, i * 4 + (k - 2 + 2 * j))
                            sp.dma_start(RAW[:, d % 2, 0:2, 0:width], source(name, i * 2 + (idx + j), 1)
                                         ).then_inc(w_raw[d % 2], 16)
                    stream(first + size - 2, 2)

            sp.dma_start(gains[:, :], I["gains"]).then_inc(sem("gains_in"), 16)
            sp.dma_start(H[:, 0:2, :], I["x"][:, 0:2, :]).then_inc(sem("x_in0"), 16)
            stream(0, 1)
            for q in range(1, 4):
                sp.dma_start(H[:, 2 * q:2 * q + 2, :], I["x"][:, 2 * q:2 * q + 2, :]).then_inc(
                    sem(f"x_in{q}"), 16)
            sp.dma_start(C[:, :], I["consts"][:, 0:kept]).then_inc(sem("consts_in"), 16)
            stream(1, 1)
            sp.dma_start(pages[:, :], I["pages"]).then_inc(sem("pages_in"), 16)
            sp.dma_start(O["win_old"], I["win_old"]).then_inc(sem("old_stored"), 16)
            stream_ffn(0, True)
            n_in = (NPROJ + 1) // 2
            mid = FFN_STEPS
            stream(mid, 3)
            sp.wait_ge(sem("rstd"), since("rstd", "a", 1))
            sp.dma_start(late[:, :], I["consts"][:, kept:ncol]).then_inc(sem("late_in"), 16)
            stream(mid + 3, n_in - 3)

            sp.wait_ge(sem("pages_in"), 16)
            page = [sp.value_load(pages[0:1, n:n + 1], min_val=0, max_val=N_POOL - 1) for n in range(NPAGE)]

            sp.wait_ge(used, IT_OUT)
            sp.wait_ge(w_hi, IT_OUT)
            sp.wait_ge(w_lo, IT_OUT)
            sp.dma_start(W2[:, :, :], I["w2"]).then_inc(sem("w2_in"), 16)
            for n in (0, 1):
                sp.dma_start(W1[n][:, :, :], I["w1"][n]).then_inc(sem(f"cmp_in{n}"), 16)
                for g in range(NPAGE):
                    sp.dma_start(X[n][:, SEQ + g * PAGE:SEQ + (g + 1) * PAGE],
                                 I["nsa_t"][bass.ds(page[g], 1), :, n, :].rearrange("a p n -> p (a n)")
                                 ).then_inc(sem(f"cmp_in{n}"), 16)
                sp.dma_start(X[n][:, SEQ + DEC * PAST:XLEN], I["pe"][n]).then_inc(sem(f"cmp_in{n}"), 16)
                sp.wait_ge(sem(f"nsa{n}_stored"), 16)
                sp.dma_start(X[n][:, 0:SEQ], O["nsa"][n, :, 0:SEQ]).then_inc(sem(f"cmp_in{n}"), 16)

            def fox_keys(b):
                for h in range(NPG):
                    sp.dma_start(KF[:, b % KF_SLOTS, :, h * PAGE:(h + 1) * PAGE],
                                 I["fox_k"][bass.ds(page[b * NPG + h], 1)].rearrange("a p t n -> p (a t) n")
                                 ).then_inc(sem(f"kf_in{b % KF_SLOTS}"), 16)

            sp.wait_ge(sem("cmp_hid"), 2)
            for b in range(KF_SLOTS):
                fox_keys(b)
            for g in range(NPAGE):
                sp.dma_start(VF[g // 8][:, g % 8, :],
                             I["fox_v"][bass.ds(page[g], 1)].rearrange("a p n -> p (a n)")
                             ).then_inc(sem("vf_in"), 16)
            sp.wait_ge(sem("att_pv"), HF + 2 * HN)
            for name in sorted({stored_sem(j) for j in STORED}):
                sp.wait_ge(sem(name), max(stored_count(j) for j in STORED if stored_sem(j) == name))
            for g in range(NPAGE):
                b, h = g // NPG, g % NPG
                sp.dma_start(LFS[HF * b:HF * b + HF, h * PAGE:(h + 1) * PAGE],
                             I["fox_lf"][bass.ds(page[g], 1)].rearrange("a p n -> (a p) n")
                             ).then_inc(sem("lf_in"), 16)
            for g in range(NPAGE):
                b, h = g // NPG, g % NPG
                sp.dma_start(KD[:, b, h * PAGE:(h + 1) * PAGE],
                             I["nsa_t"][bass.ds(page[g], 1), :, 2, :].rearrange("a p n -> p (a n)")
                             ).then_inc(sem("kd_in"), 16)
            for b in range(KF_SLOTS, DEC):
                sp.wait_ge(sem("kf_scored"), b + 1 - KF_SLOTS)
                fox_keys(b)
            for g in range(NPAGE):
                sp.dma_start(VS[:, g, :],
                             I["nsa_v"][bass.ds(page[g], 1)].rearrange("a p n -> p (a n)")
                             ).then_inc(sem("vs_in"), 16)
            sp.dma_start(VW[:, :, :], I["win_v"]).then_inc(sem("vw_in"), 16)
            sp.wait_ge(sem("cmp_pv"), 4)
            sp.dma_start(KW[:, :, 0:PAST], I["win_k"]).then_inc(sem("kw_in"), 16)

            sp.wait_ge(sem("d_scored"), 2)
            stream(mid + n_in, KT // 2)
            stream_ffn(1, False)
            sp.wait_ge(sem("y_stored"), 16 * KT)
            sp.wait_ge(sem("lf_stored"), 16)
            sp.wait_ge(sem("old_stored"), 16)

        @block.scalar
        def _(act):
            split, split_behind = splitter(act, "hi")

            def finished(s, t, par, number):
                if number is None or number >= 2:
                    act.wait_ge(sem("acc"), since("acc", s, t - 1))
                nc.scalar.activation(SQ[:, par, :], row(Y, t), ACT.Square).then_inc(sem("ysq"), 1)
                act.wait_ge(sem("ysq"), since("ysq", s, t + 1))
                g = KT * GAINS.index(POST[s])
                col = gains[:, bass.ds(t + g, 1)] if number is None else gains[:, t + g:t + g + 1]
                nc.scalar.activation(row(Y, t), row(Y, t), ACT.Copy, scale=col).then_inc(sem("yg"), 1)

            def rstd(s, kind, factor, dst, done):
                if kind == "yss" or s == "0":
                    nc.scalar.preload_act_table_set("natural_log_exp_and_others")
                act.wait_ge(sem(kind), since(kind, s, 1))
                e = 1 if factor == 4 else 0
                nc.scalar.activation(two(ST[:, 0, :]), halves(2), ACT.Ln, scale=factor / D_MODEL,
                                     bias=const("eps")[:, e:e + 1]).then_inc(sem(kind + "_ln"), 1)
                act.wait_ge(sem(kind + "_ln"), since(kind + "_ln", s, 1))
                nc.scalar.activation(dst, ST[:, 0, :], ACT.Exp, scale=-0.5).then_inc(sem(done), 1)

            def operands(s, name, arrived):
                for t in range(KT):
                    arrived(t)
                    nc.scalar.activation(XH[:, t, :], H[:, t, :], ACT.Copy, scale=gain(name, t)).then_inc(
                        sem("xhi"), 1)
                    nc.scalar.activation(Y[:, t, :], H[:, t, :], ACT.Square).then_inc(sem("hsq"), 1)
                rstd(s, "hss", 1, R1[:, :], "rstd")

            def after(s, name):
                rstd(s, "yss", 4 if s in "ac" else 1, GT[:, 0, :], "yrstd")
                if name is None:
                    return
                operands(s, name, lambda t: act.wait_ge(sem("mixed"), since("mixed", s, t + 1)))

            def ffn(f, s):
                def body(st):
                    split_behind(f, st, 0)
                    if st.kind == "gu":
                        act.wait_ge(sem("evac"), since("evac", f, st.M * 2 + 1))
                        if st.number is None or st.gate >= 2:
                            act.wait_ge(sem("hid"), since("hid", f, st.gate - 1))
                        nc.scalar.activation(ST[:, st.par, :], GT[:, st.par, :], ACT.Silu).then_inc(
                            sem("silu"), 1)
                    split_behind(f, st, 1)
                    if st.kind == "gu":
                        act.wait_ge(sem("hid"), since("hid", f, st.gate + 1))
                        nc.scalar.copy(row(UH, st.m), HT[:, st.par, :]).then_inc(sem("hid_hi"), 1)
                    elif st.g == 1:
                        act.wait_ge(sem("evac"), since("evac", f, st.M * 2 + 2))
                        finished(s, st.m, st.par, st.number)

                run_ffn(act, body)

            act.wait_ge(sem("gains_in"), 16)
            split(0)

            def arrived(t):
                act.wait_ge(sem(f"x_in{t // 2}"), 16)
                if t == 3:
                    split(1)
                if t == 7:
                    act.wait_ge(sem("consts_in"), 16)

            operands("0", "ffn1_pre", arrived)
            ffn(0, "a")
            after("a", "mix_pre")

            def stacks(j):
                kind = TILES[j]
                if kind not in STACKED:
                    return
                t = j - TILES.index(kind)
                src = RO[:, of_kind(j, ROPED) % 2, :] if kind in ROPED else TR[:, j % 4, :]
                if kind in ("fq", "nq"):
                    for h in range(2):
                        for half in range(2):
                            nc.scalar.mul(QST[64 * half:64 * half + 64, 2 * t + h, 0, :],
                                          src[64 * h:64 * h + 64, 0:SEQ], SCALE)
                    new = fq_new if kind == "fq" else nq_new
                    nc.scalar.mul(new[:, t, :], src[:, SEQ:TOK], SCALE).then_inc(sem("stack_hi"), 1)
                    return
                first = 2 * t if kind == "fk" else 2 * ("slck", "wink").index(kind)
                for h in range(2):
                    nc.scalar.copy(KST[64 * h:64 * h + 64, first + h, :], src[64 * h:64 * h + 64, 0:SEQ])
                new = fk_new[:, t, :] if kind == "fk" else nk_new[:, ("slck", "wink").index(kind), :]
                nc.scalar.copy(new, src[:, SEQ:TOK]).then_inc(sem("stack_hi"), 1)

            def store(j):
                if j in STORED:
                    name, n = STORED[j]
                    src = RO[:, of_kind(j, ROPED) % 2, :] if TILES[j] in ROPED else TR[:, j % 4, :]
                    act.dma_start(O[name][n], src).then_inc(sem(stored_sem(j)), 16)

            def late_part(j):
                kind = TILES[j]
                if kind in ROPED:
                    act.wait_ge(sem("roped"), of_kind(j, ROPED) + 1)
                    stacks(j)
                    store(j)
                elif kind in AUXED:
                    act.wait_ge(sem("turned"), of_kind(j, AUXED) + 1)
                    turned = ps[:, 4, :].rearrange("p (a n) -> p a n", a=QT)
                    if kind == "fg":
                        nc.scalar.activation(gates[:, :, :], turned[:, :, 0:24], ACT.Sigmoid)
                        act.wait_ge(sem("new_cleared"), 1)
                        nc.scalar.activation(fg_new[0:24, :], TR[0:24, 0, SEQ:TOK], ACT.Sigmoid).then_inc(
                            sem("turned_out"), 1)
                        return
                    c = 128 * of_kind(j, ("fv",)) if kind == "fv" else 128 * ("slcv", "winv").index(kind)
                    nc.scalar.copy(VT[:, :, c:c + P], turned)
                    n = c if kind == "fv" else 512 + c
                    nc.scalar.copy(v_new[:, n:n + P], ps[0:DEC, 5, 0:P]).then_inc(sem("turned_out"), 1)

            def softplus():
                act.wait_ge(sem("lf_abs"), 1)
                nc.scalar.activation(LF[2][32:40, :], LF[1][32:40, :], ACT.Exp, scale=-1.0).then_inc(
                    sem("lf_exp"), 1)
                act.wait_ge(sem("lf_exp"), 1)
                nc.scalar.activation(LF[3][32:40, :], LF[2][32:40, :], ACT.Ln,
                                     bias=ones[32:40, 0:1]).then_inc(sem("lf_ln"), 1)

            def forget_out():
                act.wait_ge(sem("lf_done"), 1)
                act.dma_start(O["logf"], LF[4][32:40, :]).then_inc(sem("lf_stored"), 16)
                act.wait_ge(sem("new_cleared"), 1)
                nc.scalar.copy(fg_new[32:40, :], LF[4][32:40, SEQ:TOK]).then_inc(sem("lf_new"), 1)

            def project(j0, j1):
                for j in range(j0, j1):
                    if j + 2 < NPROJ:
                        split(IT_PROJ + j + 2)
                    act.wait_ge(sem("projected"), j + 1)
                    kind = TILES[j]
                    if kind != "fg" and kind not in ROPED:
                        stacks(j)
                        store(j)
                    if j > j0:
                        late_part(j - 1)
                    if j == 1:
                        softplus()
                    elif j == 2:
                        forget_out()
                late_part(j1 - 1)

            def pair_out(t):
                act.wait_ge(sem("att_pv"), runs_of_pair(t)[-1] + 1)
                nc.scalar.copy(OT[:, t, 0:SEQ], ps[:, 6 + t % 2, :]).then_inc(sem("att_out"), 1)

            def attention(u0, u1, pairs):
                pairs = list(pairs)
                for v in range(u0, u1 + 3):
                    if v < u1:
                        W = P * (unit(v)[3] + 1)
                        act.wait_ge(sem("att_max"), v + 1)
                        if v >= 4:
                            act.wait_ge(sem("att_turned"), v - 3)
                        nc.scalar.activation(PR[:, v % 4, 0:W], ps[:, score_bank(v), 0:W], ACT.Exp,
                                             bias=row_max[:, v:v + 1], accum_out=row_sum[:, v:v + 1]).then_inc(
                            sem("att_exp"), 1)
                    w = v - 3
                    if w >= u0 and w % 2:
                        turn_out(act, nc.scalar.copy, w, "att_odd_out")
                    if pairs and w > 4 * runs_of_pair(pairs[0])[-1] + 6:
                        pair_out(pairs.pop(0))
                for t in pairs:
                    pair_out(t)

            project(0, NB1)
            attention(0, 4 * HF, range(4))
            project(NB1, NPROJ)
            for n in (0, 1):
                act.wait_ge(sem(f"r_stored{n}"), max(stored_count(j) for j in STORED
                                                     if stored_sem(j) == f"r_stored{n}"))
            act.wait_ge(sem("nsa0_stored"), 16)
            act.wait_ge(sem("stack_lo"), of_kind(NPROJ, STACKED))
            attention(4 * HF, 96, range(4, 8))

            for n in (0, 1):
                act.wait_ge(sem("hid_out"), n + 1)
                nc.scalar.activation(HID[n][:, 0:N_WIN - 1], HID[n][:, 0:N_WIN - 1], ACT.Gelu_apprx_tanh,
                                     bias=HID[n][:, N_WIN - 1:N_WIN]).then_inc(sem("cmp_gelu"), 1)
            act.wait_ge(sem("cmp_kv"), 1)
            act.wait_ge(sem("kc_cleared"), 1)
            for kv in range(HKV):
                nc.scalar.copy(KCS[64 * kv:64 * kv + 64, kv, 0:32],
                               ps[64 * kv:64 * kv + 64, 0, 0:32]).then_inc(sem("kc_hi"), 1)
            nc.scalar.copy(kc_new[:, :], ps[:, 0, 32:160]).then_inc(sem("kc_new"), 1)
            act.wait_ge(sem("cmp_kv"), 3)
            nc.scalar.copy(vc_new[:, :], ps[:, 2, 0:P]).then_inc(sem("vc_new"), 1)
            for h in range(HN):
                act.wait_ge(sem("cmp_scored"), h + 1)
                nc.scalar.copy(SCT[32 * (h % 4):32 * (h % 4) + 32, h // 4, :],
                               ps[0:32, h % 4, :]).then_inc(sem("cmp_sct"), 1)
            act.wait_ge(sem("cmp_shift"), 1)
            nc.scalar.activation(PC[:, :, :, :], SCM[:, :, :, :], ACT.Exp).then_inc(sem("cmp_exp"), 1)
            for g in (0, 1):
                act.wait_ge(sem("cmp_back"), g + 1)
                nc.scalar.copy(PCT[:, g, :], ps[:, 6 + g, :]).then_inc(sem("cmp_pct"), 1)

            for n, (a, b) in enumerate(((0, NEWK), (0, NEWK), (0, NEWK), (NEWK, KCMP))):
                act.wait_ge(sem("d_max"), (1, 3, 4, 4)[n])
                dst = SC[n] if n < 3 else SC[1]
                src = SC[0][:, :] if n == 0 else ps[0:ROWS, 3 if n == 2 else 2, a:b]
                nc.scalar.activation(dst[:, a:b], src, ACT.Exp, bias=dmax[:, n:n + 1],
                                     accum_out=dsum[:, n:n + 1]).then_inc(sem("d_exp"), 1)
            for n in range(3):
                act.wait_ge(sem("d_turned"), n + 1)
                for g in range(NPG):
                    act.wait_ge(sem(f"pz_cleared{n}"), 1)
                    q = nc.scalar.copy(view(PZ[n][:, g, :], 0, [[ROWS + HF, DEC], [1, HF]]),
                                       ps[:, 4 + n % 2, g * ROWS:(g + 1) * ROWS].rearrange(
                                           "p (b h) -> p b h", b=DEC))
                q.then_inc(sem("d_pz"), 1)

            split(IT_OUT)
            split(IT_OUT + 1)
            nc.scalar.preload_act_table_set("natural_log_exp_and_others")
            act.wait_ge(sem("o_all"), 2)
            for g in (0, 1):
                for t in range(4):
                    dst = OACC[:, g, :] if t == 0 else OSQ[:, t - 1, :]
                    if g == 1 and t > 0:
                        act.wait_ge(sem("oacc"), t)
                    nc.scalar.activation(dst, OT[:, 4 * g + t, :], ACT.Square).then_inc(sem("osq"), 1)
            for g in (0, 1):
                act.wait_ge(sem("oss"), g + 1)
                nc.scalar.activation(two(OR[:, g, :]), halves(2 + g), ACT.Ln, scale=1.0 / 512,
                                     bias=const("eps")[:, 0:1]).then_inc(sem("oss_ln"), 1)
                act.wait_ge(sem("oss_ln"), g + 1)
                nc.scalar.activation(OR[:, g, :], OR[:, g, :], ACT.Exp, scale=-0.5).then_inc(sem("orstd"), 1)
            for t in range(8):
                act.wait_ge(sem("onormed"), t + 1)
                nc.scalar.activation(XH[:, t, :], OT[:, t, :], ACT.Copy, scale=gain("out", t)).then_inc(
                    sem("xhi"), 1)

            for t in range(KT):
                split(IT_OUT + t + 2)
                act.wait_ge(sem("ydone_b"), t + 1)
                finished("b", t, t % 2, t)
            after("b", "ffn2_pre")
            ffn(1, "c")
            after("c", None)
            for t in range(KT):
                act.wait_ge(sem("mixed"), since("mixed", "c", t + 1))
                act.dma_start(O["y"][:, t, :], H[:, t, :]).then_inc(sem("y_stored"), 16)


        @block.vector
        def _(dve):
            split, split_behind = splitter(dve, "lo")
            chain = [0]

            def link(ins):
                chain[0] += 1
                ins.then_inc(sem("dve_chain"), 1)
                dve.wait_ge(sem("dve_chain"), chain[0])

            def low(s, name, t):
                dve.wait_ge(sem("xhi"), since("xhi", s, t + 1))
                src = OT if s == "o" else H
                nc.vector.scalar_tensor_tensor(out=XL[:, t, :], in0=src[:, t, :], scalar=gain(name, t),
                                               in1=XH[:, t, :], op0=ALU.mult, op1=ALU.subtract).then_inc(
                    sem("xlo"), 1)

            def token_rstd(s):
                dve.wait_ge(sem("hsq"), since("hsq", s, KT))
                link(nc.vector.tensor_tensor(Y[:, 4:6, :], Y[:, 4:6, :], Y[:, 6:8, :], ALU.add))
                nc.vector.tensor_tensor(Y[:, 4, :], Y[:, 4, :], Y[:, 5, :], ALU.add).then_inc(
                    sem("hacc"), 1)
                dve.wait_ge(sem("rstd"), since("rstd", s, 1))

            def after(s, name):
                dve.wait_ge(sem("yrstd"), since("yrstd", s, 1))
                for t in range(KT + 2):
                    if t < KT:
                        dve.wait_ge(sem("yg"), since("yg", s, t + 1))
                        if t >= 2:
                            dve.wait_ge(sem("mixed"), since("mixed", s, t - 1))
                        nc.vector.tensor_tensor(UT[:, t % 2, :], Y[:, t, :], GT[:, 0, :], ALU.mult).then_inc(
                            sem("normed"), 1)
                    if t >= 2 and name:
                        low(s, name, t - 2)
                if name:
                    token_rstd(s)

            def ffn(f, s):
                def body(st):
                    k = st.M * 2 + IT_F[f]
                    if st.kind == "gu":
                        dve.wait_ge(used, k + 1)
                        nc.vector.tensor_tensor(two(GT[:, st.par, :]), halves(0), two(R1[:, :]),
                                                ALU.mult).then_inc(sem("evac"), 1)
                        split_behind(f, st, 0)
                        dve.wait_ge(used, k + 2)
                        nc.vector.tensor_tensor(two(UT[:, st.par, :]), halves(1), two(R1[:, :]),
                                                ALU.mult).then_inc(sem("evac"), 1)
                        split_behind(f, st, 1)
                        dve.wait_ge(sem("silu"), since("silu", f, st.gate + 1))
                        dve.wait_ge(sem("evac"), since("evac", f, st.M * 2 + 2))
                        if st.number is None or st.gate >= 2:
                            dve.wait_ge(sem("hid_lo"), since("hid_lo", f, st.gate - 1))
                        nc.vector.tensor_tensor(HT[:, st.par, :], ST[:, st.par, :], UT[:, st.par, :],
                                                ALU.mult).then_inc(sem("hid"), 1)
                        return
                    split_behind(f, st, 0)
                    dve.wait_ge(used, k + 2)
                    if st.g == 0:
                        nc.vector.tensor_copy(two(row(Y, st.m)), halves(st.par)).then_inc(sem("evac"), 2)
                    else:
                        nc.vector.tensor_tensor(two(row(Y, st.m)), two(row(Y, st.m)), halves(st.par),
                                                ALU.add).then_inc(sem("evac"), 2)
                    split_behind(f, st, 1)

                run_ffn(dve, body)

            split(0)
            for t in range(KT):
                low("0", "ffn1_pre", t)
                if t == 3:
                    split(1)
            token_rstd("0")
            ffn(0, "a")
            after("a", "mix_pre")

            def rope_part(j):
                r = of_kind(j, ROPED)
                dve.wait_ge(sem("turned"), of_kind(j, AUXED) + 1)
                if r >= 1:
                    dve.wait_ge(sem("roped"), r)
                nc.vector.tensor_tensor(two(RS[:, :]), halves(3), two(sin), ALU.mult).then_inc(
                    sem("rope_sin"), 1)
                dve.wait_ge(sem("rope_sin"), r + 1)
                dve.wait_ge(sem("rope_cos"), r + 1)
                before = [i for i in STORED if TILES[i] in ROPED and of_kind(i, ROPED) == r - 2]
                for i in before:
                    dve.wait_ge(sem(stored_sem(i)), stored_count(i))
                nc.vector.tensor_tensor(RO[:, r % 2, :], RC[:, :], RS[:, :], ALU.add).then_inc(sem("roped"), 1)

            def stacks(j):
                kind = TILES[j]
                if kind not in STACKED:
                    return
                t = j - TILES.index(kind)
                src = RO[:, of_kind(j, ROPED) % 2, :] if kind in ROPED else TR[:, j % 4, :]
                dve.wait_ge(sem("stack_hi"), of_kind(j, STACKED) + 1)
                if kind in ROPED:
                    dve.wait_ge(sem("roped"), of_kind(j, ROPED) + 1)
                for h in range(2):
                    part = slice(64 * h, 64 * h + 64)
                    if kind in ("fq", "nq"):
                        for half in range(2):
                            q = nc.vector.scalar_tensor_tensor(
                                out=QST[64 * half:64 * half + 64, 2 * t + h, 1, :], in0=src[part, 0:SEQ],
                                scalar=SCALE, in1=QST[part, 2 * t + h, 0, :], op0=ALU.mult, op1=ALU.subtract)
                    else:
                        n = (2 * t if kind == "fk" else 2 * ("slck", "wink").index(kind)) + h
                        q = nc.vector.tensor_tensor(KST[64 - 64 * h:128 - 64 * h, n, :], src[part, 0:SEQ],
                                                    KST[part, n, :], ALU.subtract)
                q.then_inc(sem("stack_lo"), 1)

            def forget_arguments():
                r = slice(32, 32 + HF)
                bias = gains[r, KT * len(GAINS):KT * len(GAINS) + 1]
                link(nc.vector.tensor_scalar(LF[0][r, :], TR[r, 0, :], bias, None, ALU.add))
                nc.vector.scalar_tensor_tensor(out=LF[1][r, :], in0=LF[0][r, :], scalar=-1.0, in1=LF[0][r, :],
                                               op0=ALU.mult, op1=ALU.max).then_inc(sem("lf_abs"), 1)

            def forget_gates():
                r = slice(32, 32 + HF)
                dve.wait_ge(sem("lf_ln"), 1)
                nc.vector.scalar_tensor_tensor(out=LF[4][r, :], in0=LF[0][r, :], scalar=0.0, in1=LF[3][r, :],
                                               op0=ALU.min, op1=ALU.subtract).then_inc(sem("lf_done"), 1)

            def forget_sums(step):
                r = slice(32, 32 + HF)
                if step == 0:
                    dve.wait_ge(sem("lf_done"), 1)
                    link(nc.vector.tensor_tensor_scan(LF[1][r, 0:SEQ], view(ones[r, :], 0, [[0, SEQ]]),
                                                      LF[4][r, 0:SEQ], 0.0, ALU.mult, ALU.add))
                elif step == 1:
                    link(nc.vector.tensor_copy(cum_hi[r, :], LF[1][r, 0:SEQ]))
                    dve.wait_ge(sem("new_cleared"), 1)
                    nc.vector.tensor_copy(cumb[0:HF, :], LF[1][r, 0:SEQ])
                elif step == 2:
                    link(nc.vector.tensor_tensor(LF[2][r, 0:SEQ], LF[1][r, 0:SEQ], cum_hi[r, :], ALU.subtract))
                    link(nc.vector.tensor_copy(cumb[r, :], LF[2][r, 0:SEQ]))
                else:
                    link(nc.vector.tensor_tensor(LF[3][r, 0:SEQ], LF[2][r, 0:SEQ], cumb[r, :], ALU.subtract))
                    nc.vector.tensor_copy(cumb[64:64 + HF, :], LF[3][r, 0:SEQ]).then_inc(sem("cum_ready"), 1)

            def cast_constants():
                dve.wait_ge(sem("late_in"), 16)
                nc.vector.tensor_copy(identb[:, :], ident)
                nc.vector.tensor_copy(causalb[:, :], late[:, 0:P])
                nc.vector.tensor_copy(selb[:, :], late[:, P:P + HF * P]).then_inc(sem("bf_ready"), 1)

            def project(j0, j1):
                for j in range(j0, j1 + 1):
                    if j < j1:
                        dve.wait_ge(used, IT_PROJ + j + 1)
                        if j >= 4:
                            old = j - 4
                            if old in STORED and TILES[old] not in ROPED:
                                dve.wait_ge(sem(stored_sem(old)), stored_count(old))
                            if TILES[old] in AUXED:
                                dve.wait_ge(sem("turned"), of_kind(old, AUXED) + 1)
                            if TILES[old] == "fg":
                                dve.wait_ge(sem("turned_out"), 1)
                        nc.vector.tensor_tensor(two(TR[:, j % 4, :]), halves(j % 2), two(R1[:, :]),
                                                ALU.mult).then_inc(sem("projected"), 1)
                    if j > j0 and TILES[j - 1] in ROPED:
                        rope_part(j - 1)
                    if j < min(j1, NPROJ - 2):
                        split(IT_PROJ + j + 2)
                    if j < j1:
                        dve.wait_ge(sem("projected"), j + 1)
                        if TILES[j] not in ROPED:
                            stacks(j)
                        if j == 1:
                            forget_arguments()
                        elif j == 2:
                            forget_gates()
                        elif 3 <= j < 7:
                            forget_sums(j - 3)
                        elif j == 7:
                            cast_constants()
                    if j > j0 and TILES[j - 1] in ROPED:
                        stacks(j - 1)

            def attention(u0, u1):
                for v in range(u0, u1 + 3):
                    if v < u1:
                        W = P * (unit(v)[3] + 1)
                        dve.wait_ge(sem("att_scored"), v + 1)
                        nc.vector.reduce_max(row_max[:, v:v + 1], ps[:, score_bank(v), 0:W], AX.X,
                                             negate=True).then_inc(sem("att_max"), 1)
                    u = v - 1
                    if u0 <= u < u1:
                        dve.wait_ge(sem("att_exp"), u + 1)
                        nc.vector.reciprocal(row_inv[:, u:u + 1], row_sum[:, u:u + 1]).then_inc(
                            sem("att_inv"), 1)
                        if unit(u)[3] >= DVE_SCALES:
                            scale_p(dve, nc.vector.tensor_scalar, u)
                    w = v - 3
                    if w >= u0 and w % 2 == 0:
                        turn_out(dve, nc.vector.tensor_copy, w, "att_even_out")
                    for n in (0, 1):
                        if v == HID_FROM + (n + 1) * CMP_LEN // HID_PER_UNIT:
                            dve.wait_ge(sem("cmp_hid"), n + 1)
                            nc.vector.tensor_copy(HID[n][:, :], ps[:, 3, 0:N_WIN]).then_inc(sem("hid_out"), 1)

            project(0, NB1)
            dve.wait_ge(sem("lf_stored"), 16)
            dve.wait_ge(sem("lf_new"), 1)
            attention(0, 4 * HF)
            project(NB1, NPROJ)
            dve.wait_ge(sem("turned_out"), of_kind(NPROJ, ("fg", "fv", "slcv", "winv")))
            attention(4 * HF, 96)

            dve.wait_ge(sem("qb_cleared"), 1)
            for h in range(HF):
                part = slice(64 * (h % 2), 64 * (h % 2) + 64)
                kv = slice(64 * (h // 4), 64 * (h // 4) + 64)
                nc.vector.tensor_copy(view(QBF[part, h // 2, :], h, [[ROWS + HF, DEC]]), fq_new[part, h // 2, :])
                q = nc.vector.tensor_copy(view(QBN[kv, :], h, [[ROWS + HF, DEC]]), nq_new[part, h // 2, :])
            q.then_inc(sem("qb_filled"), 1)
            for b in range(KF_SLOTS):
                nc.vector.tensor_copy(KF[:, b, :, PAST], fk_new[:, :, b]).then_inc(sem("kf_new"), 1)
            dve.wait_ge(sem("kc_hi"), HKV)
            dve.wait_ge(sem("kc_new"), 1)
            for kv in range(HKV):
                nc.vector.tensor_tensor(KCS[64 - 64 * kv:128 - 64 * kv, kv, 0:32],
                                        ps[64 * kv:64 * kv + 64, 0, 0:32],
                                        KCS[64 * kv:64 * kv + 64, kv, 0:32], ALU.subtract).then_inc(
                    sem("kc_lo"), 1)
            dve.wait_ge(sem("cmp_kv"), 2)
            dve.wait_ge(sem("vc_cleared"), 1)
            for h in range(HN):
                q = nc.vector.tensor_copy(VCZ[32 * (h % 4):32 * (h % 4) + 32, h // 2,
                                              64 * (h % 2):64 * (h % 2) + 64],
                                          ps[0:32, 1, 64 * (h // 4):64 * (h // 4) + 64])
            q.then_inc(sem("vc_placed"), 1)

            def by_tile(name):
                return view(const(name), 0, [[32, QT], [0, HN], [1, 32]])

            def by_row(t):
                return view(t[:, :, :], 0, [[HN, QT], [1, HN], [0, 32]])

            dve.wait_ge(sem("cmp_rows"), 1)
            rows = view(ps[:, 4, :], 0, [[256, QT], [32, HN], [1, 32]])
            link(nc.vector.tensor_tensor(SCM[:, :, :, :], rows, by_tile("cmask"), ALU.add))
            link(nc.vector.reduce_max(cmax[:, :, :], SCM[:, :, :, :], AX.X))
            nc.vector.tensor_tensor(SCM[:, :, :, :], SCM[:, :, :, :], by_row(cmax), ALU.subtract).then_inc(
                sem("cmp_shift"), 1)
            dve.wait_ge(sem("cmp_exp"), 1)
            link(nc.vector.reduce_sum(csum[:, :, :], PC[:, :, :, :], AX.X))
            link(nc.vector.reciprocal(csum[:, :, :], csum[:, :, :]))
            link(nc.vector.tensor_tensor(cinv[:, :, :], view(gates[:, :, :], 0, [[24, QT], [3, HN]]),
                                         csum[:, :, :], ALU.mult))
            link(nc.vector.tensor_tensor(PC[:, :, :, :], PC[:, :, :, :], by_row(cinv), ALU.mult))
            nc.vector.tensor_tensor(PC[:, :, :, :], PC[:, :, :, :], by_tile("cok"), ALU.mult).then_inc(
                sem("cmp_p"), 1)
            for b in range(KF_SLOTS, DEC):
                dve.wait_ge(sem("kf_scored"), b + 1 - KF_SLOTS)
                nc.vector.tensor_copy(KF[:, b % KF_SLOTS, :, PAST], fk_new[:, :, b]).then_inc(sem("kf_new"), 1)
            for t in range(4):
                dve.wait_ge(sem("cmp_pv"), t + 1)
                dve.wait_ge(sem("att_out"), 8)
                nc.vector.tensor_tensor(OT[:, 4 + t, 0:SEQ], OT[:, 4 + t, 0:SEQ], ps[:, 1 + t, :],
                                        ALU.add).then_inc(sem("o_cmp"), 1)

            dve.wait_ge(sem("kc_new"), 1)
            nc.vector.tensor_copy(KD[:, :, PAST], nk_new[:, 0, :])
            nc.vector.tensor_copy(KD[:, :, NEWK:KCMP], view(kc_new[:, :], 0, [[16, DEC], [1, N_CMP_S]])).then_inc(
                sem("kd_new"), 1)
            nc.vector.tensor_copy(KW[:, :, PAST], nk_new[:, 1, :]).then_inc(sem("kw_new"), 1)
            dve.wait_ge(sem("d_picked"), 1)
            link(nc.vector.tensor_tensor(GB[:, :, :], view(ps[0:ROWS, 1, :], 0, [[DEC, 4], [1, DEC]]),
                                         view(const("is_b")[0:ROWS, :], 0, [[0, 4], [1, DEC]]), ALU.mult))
            link(nc.vector.reduce_sum(picked[:, :], GB[:, :, :], AX.X))
            link(nc.vector.tensor_copy(LFS[:, PAST:NEWK], picked[:, 3:4]))
            dve.wait_ge(sem("lf_in"), 16 * NPAGE)
            link(nc.vector.tensor_tensor_scan(CUMS[:, :], view(ones[0:ROWS, :], 0, [[0, NEWK]]), LFS[:, :],
                                              0.0, ALU.mult, ALU.add))
            dve.wait_ge(sem("kf_scored"), DEC)
            link(nc.vector.tensor_tensor(SC[0][:, :], ps[0:ROWS, 0, 0:NEWK], CUMS[:, :], ALU.subtract))
            nc.vector.reduce_max(dmax[:, 0:1], SC[0][:, :], AX.X, negate=True).then_inc(sem("d_max"), 1)
            for n, bank, a, b in ((1, 2, 0, NEWK), (3, 2, NEWK, KCMP), (2, 3, 0, NEWK)):
                dve.wait_ge(sem("d_scored"), bank - 1)
                nc.vector.reduce_max(dmax[:, n:n + 1], ps[0:ROWS, bank, a:b], AX.X, negate=True).then_inc(
                    sem("d_max"), 1)
            for n, (buf, a, b) in enumerate(((0, 0, NEWK), (1, 0, NEWK), (2, 0, NEWK), (1, NEWK, KCMP))):
                dve.wait_ge(sem("d_exp"), n + 1)
                link(nc.vector.reciprocal(dinv[:, n:n + 1], dsum[:, n:n + 1]))
                c = n % 3
                gate, times = (None, {}) if n == 0 else (picked[:, c:c + 1], {"op1": ALU.mult})
                nc.vector.tensor_scalar(SC[buf][:, a:b], SC[buf][:, a:b], dinv[:, n:n + 1], gate,
                                        ALU.mult, **times).then_inc(sem("d_p"), 1)
            dve.wait_ge(sem("d_p"), 4)
            for n in range(3):
                nc.vector.tensor_scalar(PN[:, n, :], const("is_b")[0:ROWS, :], SC[n][:, PAST:NEWK], None,
                                        ALU.mult)
            link(nc.vector.memset(PCX[:, :, :], 0.0))
            nc.vector.tensor_tensor(PCX[:, :, 0:N_CMP_S],
                                    view(SC[1][:, NEWK:KCMP], 0, [[0, DEC], [1, N_CMP_S]]),
                                    view(const("is_b")[0:ROWS, :], 0, [[1, DEC], [0, N_CMP_S]]),
                                    ALU.mult).then_inc(sem("d_pn"), 1)
            dve.wait_ge(sem("d_new_turned"), 1)
            nc.vector.tensor_copy(PNT[:, :, :], ps[0:DEC, 7, 0:3 * ROWS].rearrange("p (n r) -> p n r", n=3))
            nc.vector.tensor_copy(PCZ[:, :], ps[:, 6, 0:ROWS]).then_inc(sem("d_pnt"), 1)
            dve.wait_ge(sem("d_pv"), 1)
            link(nc.vector.tensor_tensor(EF[:, :, :], view(ps[0:ROWS, 1, :], 0, [[DH, HF], [1, DH]]),
                                         view(const("is_h")[0:ROWS, :], 0, [[1, HF], [0, DH]]), ALU.mult))
            nc.vector.reduce_sum(OS[:, 0, :], view(EF[:, :, :], 0, [[1, DH], [DH, HF]]), AX.X)
            dve.wait_ge(sem("d_pv"), 2)
            link(nc.vector.tensor_tensor(EN[:, :, :], view(ps[0:ROWS, 0, :], 0, [[DH, HKV], [1, DH]]),
                                         view(const("is_kv")[0:ROWS, :], 0, [[1, HKV], [0, DH]]), ALU.mult))
            nc.vector.tensor_tensor(OS[:, 1, :], EN[:, 0, :], EN[:, 1, :], ALU.add).then_inc(sem("d_o"), 1)
            for g in (0, 1):
                dve.wait_ge(sem("d_ot"), g + 1)
                for j in (0, 1):
                    q = nc.vector.tensor_copy(
                        OT[64 * j:64 * j + 64, 4 * g:4 * g + 4, SEQ:TOK],
                        view(ps[0:DH, 4 + g, :], j, [[2, 4], [HF, DEC]]))
                q.then_inc(sem("o_all"), 1)

            split(IT_OUT)
            split(IT_OUT + 1)
            for g in (0, 1):
                for t in range(1, 4):
                    dve.wait_ge(sem("osq"), 4 * g + t + 1)
                    if g + t > 1:
                        dve.wait_ge(sem("oacc"), 3 * g + t - 1)
                    nc.vector.tensor_tensor(OACC[:, g, :], OACC[:, g, :], OSQ[:, t - 1, :], ALU.add).then_inc(
                        sem("oacc"), 1)
            for t in range(9):
                if t < 8:
                    dve.wait_ge(sem("orstd"), t // 4 + 1)
                    nc.vector.tensor_tensor(OT[:, t, :], OT[:, t, :], OR[:, t // 4, :], ALU.mult).then_inc(
                        sem("onormed"), 1)
                if t:
                    dve.wait_ge(sem("onormed"), t)
                    low("o", "out", t - 1)

            for t in range(KT):
                dve.wait_ge(used, IT_OUT + t + 1)
                nc.vector.tensor_copy(two(Y[:, t, :]), halves(t % 2)).then_inc(sem("ydone_b"), 1)
                split(IT_OUT + t + 2)
            after("b", "ffn2_pre")
            ffn(1, "c")
            after("c", None)

        @block.gpsimd
        def _(pool):
            nc.gpsimd.memset(fg_new[:, :], 0.0)
            nc.gpsimd.memset(cumb[:, :], 0.0).then_inc(sem("new_cleared"), 1)

            def accumulate(s, t, par, number):
                if number == KT - 1:
                    return
                pool.wait_ge(sem("ysq"), since("ysq", s, t + 1))
                if number == 0:
                    nc.gpsimd.tensor_copy(ACC[:, :], SQ[:, 0, :]).then_inc(sem("acc"), 1)
                    return
                pool.wait_ge(sem("acc"), since("acc", s, t))
                nc.gpsimd.tensor_tensor(ACC[:, :], ACC[:, :], SQ[:, par, :], ALU.add).then_inc(
                    sem("acc"), 1)

            def ffn(f, s):
                def body(st):
                    if st.kind == "gu":
                        pool.wait_ge(sem("hid_hi"), since("hid_hi", f, st.gate + 1))
                        nc.gpsimd.tensor_tensor(row(UL, st.m), HT[:, st.par, :], row(UH, st.m),
                                                ALU.subtract).then_inc(sem("hid_lo"), 1)
                    elif st.g == 1:
                        accumulate(s, st.m, st.par, st.number)

                run_ffn(pool, body)

            def after(s):
                for t in range(KT):
                    pool.wait_ge(sem("normed"), since("normed", s, t + 1))
                    nc.gpsimd.tensor_tensor(H[:, t, :], H[:, t, :], UT[:, t % 2, :], ALU.add).then_inc(
                        sem("mixed"), 1)

            def project(j0, j1):
                for j in range(j0, j1):
                    if TILES[j] in ROPED:
                        r = of_kind(j, ROPED)
                        pool.wait_ge(sem("projected"), j + 1)
                        if r >= 1:
                            pool.wait_ge(sem("roped"), r)
                        nc.gpsimd.tensor_tensor(RC[:, :], TR[:, j % 4, :], cos, ALU.mult).then_inc(
                            sem("rope_cos"), 1)

            def attention(u0, u1):
                for u in range(u0, u1):
                    if unit(u)[3] < DVE_SCALES:
                        scale_p(pool, nc.gpsimd.tensor_scalar, u)

            ffn(0, "a")
            after("a")
            attention(0, 4 * HF)
            project(NB1, NPROJ)
            pool.wait_ge(used, IT_OUT)
            nc.gpsimd.memset(QBF[:, :, :], 0.0)
            nc.gpsimd.memset(QBN[:, :], 0.0).then_inc(sem("qb_cleared"), 1)
            attention(4 * HF, 96)
            pool.wait_ge(sem("att_pv"), HF + 2 * HN)
            nc.gpsimd.memset(KCS[:, :, :].bitcast(F32), 0.0).then_inc(sem("kc_cleared"), 1)
            nc.gpsimd.memset(VCZ[:, :, :], 0.0).then_inc(sem("vc_cleared"), 1)
            nc.gpsimd.memset(PZ[0][:, :, :], 0.0).then_inc(sem("pz_cleared0"), 1)
            pool.wait_ge(sem("cmp_scored"), HN)
            nc.gpsimd.memset(PZ[2][:, :, :], 0.0).then_inc(sem("pz_cleared2"), 1)
            pool.wait_ge(sem("cmp_pv"), 4)
            nc.gpsimd.memset(PZ[1][:, :, :], 0.0).then_inc(sem("pz_cleared1"), 1)
            for t in range(KT):
                accumulate("b", t, t % 2, t)
            after("b")
            ffn(1, "c")
            after("c")

        @block.tensor
        def _(pe):
            def ready(k):
                pe.wait_ge(w_hi, k + 1)
                pe.wait_ge(w_lo, k + 1)

            def products(par, n, xh, xl, slot, first=True, last=True, kt0=0, arrived=None):
                for kt in range(n):
                    if arrived:
                        arrived(kt)
                    cols = slice(kt * P, kt * P + P)
                    for p, (w, x) in enumerate(((WH, xh), (WH, xl), (WL, xh))):
                        for half in (0, 1):
                            q = nc.tensor.matmul(ps[:, 2 * slot + half, 0:HALF], w[:, par, cols],
                                                 x[:, kt0 + kt, half * HALF:(half + 1) * HALF],
                                                 start=first and kt == 0 and p == 0,
                                                 stop=last and kt == n - 1 and p == 2)
                q.then_inc(used, 1)

            def all_partitions(src, slot, start=True, stop=True):
                for half in (0, 1):
                    q = nc.tensor.matmul(ps[:, 2 * slot + half, 0:HALF], ones,
                                         src[:, half * HALF:(half + 1) * HALF], start=start, stop=stop)
                return q

            def keep_warm(count, bank=7):
                for _ in range(count):
                    nc.tensor.matmul(ps[:, bank, :], cumb[:, 0:P], cumb[:, :], start=True, stop=True)

            def first_operands(s, kt):
                if kt >= KT - HSQ_PE:
                    t = kt - (KT - HSQ_PE)
                    if t == 0 and s == "0":
                        pe.wait_ge(sem("consts_in"), 16)
                    pe.wait_ge(sem("hsq"), since("hsq", s, t + 1))
                    all_partitions(Y[:, t, :], 2, start=t == 0, stop=False)
                pe.wait_ge(sem("xlo"), since("xlo", s, kt + 1))

            def token_squares(s, kt):
                if kt == HSS_AT:
                    pe.wait_ge(sem("hacc"), since("hacc", s, 1))
                    all_partitions(Y[:, HSQ_PE, :], 2, start=False).then_inc(sem("hss"), 1)

            def output_squares(s):
                pe.wait_ge(sem("acc"), since("acc", s, KT - 1))
                all_partitions(ACC[:, :], 2, stop=False)
                pe.wait_ge(sem("ysq"), since("ysq", s, KT))
                all_partitions(SQ[:, (KT - 1) % 2, :], 2, start=False).then_inc(sem("yss"), 1)

            def ffn(f, before, s):
                def body(st):
                    k = st.M * 2 + IT_F[f]
                    known = st.number
                    if st.kind == "gu":
                        first = known == 0 and st.g == 0
                        ready(k)
                        if not first:
                            pe.wait_ge(sem("evac"), since("evac", f, st.M * 2 - (2 if known == 0 else 1)))
                        products(IT_F[f] % 2, KT, XH, XL, 0,
                                 arrived=(lambda kt: first_operands(before, kt)) if first else None)
                        ready(k + 1)
                        if not first:
                            pe.wait_ge(sem("evac"), since("evac", f, st.M * 2))
                        products((IT_F[f] + 1) % 2, KT, XH, XL, 1,
                                 arrived=(lambda kt: token_squares(before, kt)) if first else None)
                        return
                    n = GROUPS[st.g] // 2
                    if known == 0:
                        pe.wait_ge(sem("evac"), since("evac", f, st.M * 2 - 1))
                    else:
                        pe.wait_ge(sem("evac"), since("evac", f, st.M * 2 - 2))
                    hidden = sum(GROUPS[:st.g])
                    for e in (0, 1):
                        arrived = None
                        if known == 0:
                            arrived = lambda kt, e=e: pe.wait_ge(sem("hid_lo"), since("hid_lo", f, hidden + e * n + kt + 1))
                        ready(k + e)
                        products((IT_F[f] + e) % 2, n, UH, UL, st.par, first=e == 0, last=e == 1, kt0=e * n,
                                 arrived=arrived)

                run_ffn(pe, body)
                output_squares(s)

            pe.wait_ge(sem("new_cleared"), 1)
            keep_warm(WARM[0])
            ffn(0, "0", "a")
            keep_warm(WARM[1])

            def turn(j):
                kind = TILES[j]
                if kind not in AUXED:
                    return
                src = TR[:, j % 4, :]
                pe.wait_ge(sem("projected"), j + 1)
                if kind in ROPED:
                    if of_kind(j, ROPED):
                        pe.wait_ge(sem("rope_sin"), of_kind(j, ROPED))
                    for half in (0, 1):
                        q = nc.tensor.matmul(ps[:, 6 + half, 0:HALF], const("rot"),
                                             src[:, half * HALF:(half + 1) * HALF], start=True, stop=True)
                    q.then_inc(sem("turned"), 1)
                    return
                n = of_kind(j, ("fg", "fv", "slcv", "winv"))
                if n:
                    pe.wait_ge(sem("turned_out"), n)
                if kind != "fg":
                    nc.tensor.transpose(ps[0:DEC, 5, 0:P], src[:, SEQ:TOK], ident)
                for i in range(QT):
                    q = nc.tensor.transpose(ps[:, 4, i * P:i * P + P], src[:, i * P:i * P + P], ident)
                q.then_inc(sem("turned"), 1)

            def project(j0, j1):
                for j in range(j0, j1):
                    ready(IT_PROJ + j)
                    if j >= 2:
                        pe.wait_ge(sem("projected"), j - 1)
                    arrived = {0: lambda kt: first_operands("a", kt), 1: lambda kt: token_squares("a", kt)}.get(j)
                    products((IT_PROJ + j) % 2, KT, XH, XL, j % 2, arrived=arrived)
                    if j > j0:
                        turn(j - 1)
                turn(j1 - 1)

            def scores(v):
                fox, h, br, i, _ = unit(v)
                W = P * (i + 1)
                n = max(W, 2 * P)
                k = h if fox else 2 * br + h // 4
                banks = 4 if fox else 3
                if v >= banks:
                    pe.wait_ge(sem("att_exp"), v - banks + 1)
                bank = ps[:, score_bank(v), :]
                for part in (0, 1):
                    nc.tensor.matmul(bank[:, 0:n], QST[:, h, part, i * P:i * P + P], KST[:, k, 0:n],
                                     start=part == 0, stop=False, skip_group_check=True)
                if fox:
                    nc.tensor.matmul(bank[:, 0:W], selb[:, h * P:h * P + P], cumb[:, 0:W],
                                     start=False, stop=False, skip_group_check=True)
                nc.tensor.matmul(bank[:, W - P:W], identb[:, :], causalb[:, :], start=False, stop=True,
                                 skip_group_check=True).then_inc(sem("att_scored"), 1)

            def turn_p(w):
                i = unit(w)[3]
                pe.wait_ge(sem(scaled_by(w)), scaled_count(w))
                if w >= 2:
                    pe.wait_ge(sem("att_odd_out" if w % 2 else "att_even_out"), w // 2)
                for kb in range(i + 1):
                    q = nc.tensor.transpose(ps[:, 4 + w % 2, kb * P:kb * P + P],
                                            PR[:, w % 4, kb * P:kb * P + P], ident)
                q.then_inc(sem("att_turned"), 1)

            def weigh(run, kb):
                fox, h, br, _, _ = unit(4 * run)
                t, j = (h // 2) + (0 if fox else 4), h % 2
                c = h * DH if fox else br * P + (h // 4) * DH
                if kb == 0:
                    pe.wait_ge(sem("att_even_out"), 2 * run + 2)
                    pe.wait_ge(sem("att_odd_out"), 2 * run + 2)
                    if t >= 2 and j == 0 and br == 0:
                        pe.wait_ge(sem("att_out"), t - 1)
                q = nc.tensor.matmul(ps[64 * j:64 * j + 64, 6 + t % 2, kb * P:SEQ], VT[:, kb, c:c + DH],
                                     PTS[:, run % 2, kb, kb * P:SEQ], start=kb == 0 and br == 0,
                                     stop=kb == QT - 1 and (fox or br == 1), skip_group_check=True)
                if kb == QT - 1:
                    q.then_inc(sem("att_pv"), 1)

            def windows(step):
                for k in range(step * HID_PER_UNIT, (step + 1) * HID_PER_UNIT):
                    n, j = k // CMP_LEN, k % CMP_LEN
                    if j == 0:
                        pe.wait_ge(sem(f"cmp_in{n}"), 16 * (3 + NPAGE))
                        if n:
                            pe.wait_ge(sem("hid_out"), 1)
                    q = nc.tensor.matmul(ps[:, 3, 0:N_WIN], W1[n][:, j, :],
                                         view(X[n][:, :], j, [[CMP_STRIDE, N_WIN]]),
                                         start=j == 0, stop=j == CMP_LEN - 1)
                    if j == CMP_LEN - 1:
                        q.then_inc(sem("cmp_hid"), 1)

            def attention(u0, u1):
                parts = [(run, kb) for run in range(u0 // 4, u1 // 4) for kb in range(QT)]
                for v in range(u0, u1 + 3):
                    if v < u1:
                        scores(v)
                    if v - 3 >= u0:
                        turn_p(v - 3)
                    if v >= 4 * parts[0][0] + 8:
                        weigh(*parts.pop(0))
                    if HID_FROM <= v < HID_FROM + 2 * CMP_LEN // HID_PER_UNIT:
                        windows(v - HID_FROM)
                for run, kb in parts:
                    weigh(run, kb)

            project(0, NB1)
            pe.wait_ge(sem("stack_lo"), of_kind(NB1, STACKED))
            pe.wait_ge(sem("projected"), NB1)
            pe.wait_ge(sem("turned_out"), of_kind(NB1, ("fg", "fv", "slcv", "winv")))
            pe.wait_ge(sem("cum_ready"), 1)
            pe.wait_ge(sem("bf_ready"), 1)
            attention(0, 4 * HF)
            pe.wait_ge(sem("att_out"), 4)
            pe.wait_ge(sem("att_even_out"), 2 * HF)
            project(NB1, NPROJ)
            pe.wait_ge(sem("stack_lo"), of_kind(NPROJ, STACKED))
            pe.wait_ge(sem("projected"), NPROJ)
            pe.wait_ge(sem("turned_out"), of_kind(NPROJ, ("fg", "fv", "slcv", "winv")))
            attention(4 * HF, 96)

            pe.wait_ge(sem("w2_in"), 16)
            pe.wait_ge(sem("cmp_gelu"), 1)
            nc.tensor.matmul(ps[:, 0, 0:N_WIN - 1], W2[:, 0, :], HID[0][:, 0:N_WIN - 1],
                             start=True, stop=True).then_inc(sem("cmp_kv"), 1)
            pe.wait_ge(sem("cmp_gelu"), 2)
            nc.tensor.matmul(ps[0:32, 1, 0:P], HID[1][:, 0:32], W2[:, 1, :],
                             start=True, stop=True).then_inc(sem("cmp_kv"), 1)
            nc.tensor.matmul(ps[:, 2, 0:P], HID[1][:, 32:160], W2[:, 1, :],
                             start=True, stop=True).then_inc(sem("cmp_kv"), 1)
            pe.wait_ge(sem("kc_lo"), 2)
            pe.wait_ge(sem("kc_new"), 1)
            pe.wait_ge(sem("vc_placed"), 1)
            pe.wait_ge(sem("vc_new"), 1)
            for h in range(HN):
                if h >= 4:
                    pe.wait_ge(sem("cmp_sct"), h - 3)
                for part in (0, 1):
                    q = nc.tensor.matmul(ps[:, h % 4, :], KCS[:, h // 4, :], QST[:, h, part, :],
                                         start=part == 0, stop=part == 1)
                q.then_inc(sem("cmp_scored"), 1)
            pe.wait_ge(sem("cmp_sct"), HN)
            for i in range(QT):
                for g in (0, 1):
                    q = nc.tensor.transpose(ps[:, 4 + i // 2, (i % 2) * 256 + g * P:(i % 2) * 256 + g * P + P],
                                            SCT[:, g, i * P:i * P + P], ident)
            q.then_inc(sem("cmp_rows"), 1)
            pe.wait_ge(sem("qb_filled"), 1)
            for b in range(DEC):
                pe.wait_ge(sem(f"kf_in{b % KF_SLOTS}"), 16 * NPG * (b // KF_SLOTS + 1))
                pe.wait_ge(sem("kf_new"), b + 1)
                for t in range(4):
                    q = nc.tensor.matmul(ps[0:ROWS, 0, 0:NEWK], QBF[:, t, b * ROWS:(b + 1) * ROWS],
                                         KF[:, b % KF_SLOTS, t, :], start=b + t == 0,
                                         stop=b == DEC - 1 and t == 3)
                q.then_inc(sem("kf_scored"), 1)
            pe.wait_ge(sem("cmp_p"), 1)
            for g in (0, 1):
                for i in range(QT):
                    q = nc.tensor.transpose(ps[:, 6 + g, i * P:i * P + P],
                                            PC[:, i, 4 * g:4 * g + 4, :].rearrange("p h n -> p (h n)"), ident)
                q.then_inc(sem("cmp_back"), 1)
            for t in range(4):
                pe.wait_ge(sem("cmp_pct"), t // 2 + 1)
                nc.tensor.matmul(ps[:, 1 + t, :], VCZ[:, t, :], PCT[:, t // 2, :], start=True, stop=True).then_inc(
                    sem("cmp_pv"), 1)

            pe.wait_ge(sem("o_cmp"), 4)
            pe.wait_ge(sem("lf_new"), 1)
            for c in range(4):
                q = nc.tensor.matmul(ps[0:ROWS, 1, c * DEC:(c + 1) * DEC],
                                     const("pick")[0:64, c * ROWS:(c + 1) * ROWS], fg_new[0:64, :],
                                     start=True, stop=True)
            q.then_inc(sem("d_picked"), 1)
            pe.wait_ge(sem("kd_in"), 16 * NPAGE)
            pe.wait_ge(sem("kd_new"), 1)
            for b in range(DEC):
                q = nc.tensor.matmul(ps[0:ROWS, 2, 0:KCMP], QBN[:, b * ROWS:(b + 1) * ROWS], KD[:, b, :],
                                     start=b == 0, stop=b == DEC - 1)
            q.then_inc(sem("d_scored"), 1)
            pe.wait_ge(sem("kw_in"), 16)
            pe.wait_ge(sem("kw_new"), 1)
            for b in range(DEC):
                q = nc.tensor.matmul(ps[0:ROWS, 3, 0:NEWK], QBN[:, b * ROWS:(b + 1) * ROWS], KW[:, b, :],
                                     start=b == 0, stop=b == DEC - 1)
            q.then_inc(sem("d_scored"), 1)
            for n in range(3):
                pe.wait_ge(sem("d_p"), n + 1)
                if n == 2:
                    pe.wait_ge(sem("d_pz"), 1)
                for g in range(NPG):
                    q = nc.tensor.transpose(ps[:, 4 + n % 2, g * ROWS:(g + 1) * ROWS],
                                            SC[n][:, g * PAGE:(g + 1) * PAGE], ident[0:ROWS, 0:ROWS])
                q.then_inc(sem("d_turned"), 1)
            pe.wait_ge(sem("d_pn"), 1)
            for n in range(3):
                nc.tensor.transpose(ps[0:DEC, 7, n * ROWS:(n + 1) * ROWS], PN[:, n, :], ident[0:ROWS, 0:ROWS])
            nc.tensor.transpose(ps[:, 6, 0:ROWS], PCX[:, :, :].rearrange("p b n -> p (b n)"),
                                ident[0:ROWS, 0:ROWS]).then_inc(sem("d_new_turned"), 1)
            pe.wait_ge(sem("d_pz"), 1)
            pe.wait_ge(sem("d_pnt"), 1)
            pe.wait_ge(sem("vf_in"), 16 * NPAGE)
            for g in range(NPAGE):
                nc.tensor.matmul(ps[0:ROWS, 1, :], PZ[0][:, g % NPG, (g // NPG) * ROWS:(g // NPG + 1) * ROWS],
                                 VF[g // 8][:, g % 8, :], start=g == 0, stop=False)
            nc.tensor.matmul(ps[0:ROWS, 1, :], PNT[:, 0, :], v_new[:, 0:512], start=False,
                             stop=True).then_inc(sem("d_pv"), 1)
            pe.wait_ge(sem("d_pz"), 3)
            pe.wait_ge(sem("vs_in"), 16 * NPAGE)
            pe.wait_ge(sem("vw_in"), 16)
            for n, V in ((1, VS), (2, VW)):
                for g in range(NPAGE):
                    nc.tensor.matmul(ps[0:ROWS, 0, 0:P],
                                     PZ[n][:, g % NPG, (g // NPG) * ROWS:(g // NPG + 1) * ROWS],
                                     V[:, g, :], start=n == 1 and g == 0, stop=False)
                nc.tensor.matmul(ps[0:ROWS, 0, 0:P], PNT[:, n, :], v_new[:, 384 + n * P:512 + n * P],
                                 start=False, stop=False)
            nc.tensor.matmul(ps[0:ROWS, 0, 0:P], PCZ[:, :], vc_new[:, :], start=False, stop=True).then_inc(
                sem("d_pv"), 1)
            pe.wait_ge(sem("d_o"), 1)
            for g in (0, 1):
                nc.tensor.transpose(ps[0:DH, 4 + g, 0:ROWS], OS[:, g, :],
                                    ident[0:ROWS, 0:ROWS]).then_inc(sem("d_ot"), 1)

            pe.wait_ge(sem("o_all"), 2)
            for g in (0, 1):
                pe.wait_ge(sem("oacc"), 3 * g + 3)
                all_partitions(OACC[:, g, :], 2 + g).then_inc(sem("oss"), 1)
            keep_warm(WARM[2], bank=0)
            for t in range(KT):
                ready(IT_OUT + t)
                if t >= 2:
                    pe.wait_ge(sem("ydone_b"), t - 1)
                arrived = (lambda kt: pe.wait_ge(sem("xlo"), since("xlo", "o", kt + 1))) if t == 0 else None
                products((IT_OUT + t) % 2, KT, XH, XL, t % 2, arrived=arrived)
            output_squares("b")
            keep_warm(WARM[1])
            ffn(1, "b", "c")


def positions():
    inv = (np.float32(THETA) ** (-np.arange(DH // 2, dtype=np.float32) / np.float32(DH // 2))).astype(np.float32)
    pos = np.concatenate([np.arange(SEQ), np.full(DEC, PAST)]).astype(np.float32)
    ang = np.tile(inv, P // (DH // 2))[:, None] * pos[None, :]
    rot = np.zeros((P, P), np.float32)
    for m in range(P):
        low = m % DH < DH // 2
        rot[m + (DH // 2 if low else -(DH // 2)), m] = -1.0 if low else 1.0
    return np.cos(ang).astype(np.float32), np.sin(ang).astype(np.float32), rot


def constants():
    cc, n = const_columns()
    out = np.zeros((P, n), np.float32)
    cos, sin, rot = positions()
    p = np.arange(P)
    query = (np.arange(QT)[None, :, None] * P + p[:, None, None])
    end = np.arange(32)[None, None, :] * CMP_STRIDE + CMP_LEN - 1
    ok = ((end <= query) & (np.arange(32) < N_CMP)[None, None, :]).astype(np.float32).reshape(P, QT * 32)
    pick = np.zeros((P, 4, DEC, HF), np.float32)
    sel = np.zeros((P, HF, P), np.float32)
    for h in range(HF):
        for c in range(3):
            pick[3 * h + c, c, :, h] = 1.0
        pick[32 + h, 3, :, h] = 1.0
        for part in range(3):
            sel[32 * part + h, h, :] = -1.0
    values = {
        "ident": np.eye(P), "ones": np.ones((P, P)), "rot": rot, "cos": cos, "sin": sin,
        "cmask": np.where(ok > 0, 0.0, NEG), "cok": ok, "pick": pick.reshape(P, -1),
        "is_h": (p % HF)[:, None] == np.arange(HF), "is_b": (p // HF)[:, None] == np.arange(DEC),
        "is_kv": ((p % HF) // (HN // HKV))[:, None] == np.arange(HKV),
        "eps": np.tile([EPS, 4 * EPS], (P, 1)),
        "causal": np.where(p[None, :] <= p[:, None], 0.0, NEG), "sel": sel.reshape(P, -1)}
    for name, (a, b) in cc.items():
        out[:, a:b] = values[name]
    return out


def lay_out(x):
    def get(name):
        return np.asarray(x[name])

    def items(w):
        k, n = w.shape
        return w.reshape(k // P, P, n // P, P).transpose(2, 1, 0, 3)

    out = {"consts": constants()}
    tokens = np.concatenate([get("x_prompt")[0], get("x_sample")[:, 0]], axis=0)
    out["x"] = tokens.T.reshape(KT, P, TOK).transpose(1, 0, 2)
    cols = [get("g_" + n)[0].reshape(KT, P).T for n in ("ffn1_pre", "ffn1_post", "mix_pre")]
    cols.append(np.concatenate([get("g_fox_out")[0], get("g_nsa_out")[0]]).reshape(KT, P).T)
    cols += [get("g_" + n)[0].reshape(KT, P).T for n in ("mix_post", "ffn2_pre", "ffn2_post")]
    bias = np.zeros((P, 1), np.float32)
    bias[32:32 + HF, 0] = get("b_fox_f")[0]
    out["gains"] = np.concatenate(cols + [bias], axis=1)
    for f in (1, 2):
        gu = np.stack([items(get(f"w_ffn{f}_gate")[0]), items(get(f"w_ffn{f}_up")[0])], axis=2)
        out[f"w_gu{f}"] = gu.reshape(FT, P, 2, KT * P)
        down, r = get(f"w_ffn{f}_down")[0], 0
        for g, size in enumerate(GROUPS):
            part = items(down[r:r + size * P])
            out[f"w_down{f}{g}"] = part.reshape(KT, P, 2, size // 2 * P)
            r += size * P
    w = get("w_in")[0]
    fox = 3 * HF * DH
    nq = fox + HF
    kv = nq + HN * DH
    ng = kv + 6 * HKV * DH
    fg = np.zeros((D_MODEL, P), np.float32)
    fg[:, 0:3 * HN] = w[:, ng:ng + 3 * HN]
    fg[:, 32:32 + HF] = w[:, fox:fox + HF]
    order = [0, 2, 4, 1, 3, 5]
    tiles = [fg, w[:, 0:fox], w[:, nq:kv]] + [w[:, kv + P * n:kv + P * n + P] for n in order]
    out["w_in"] = items(np.concatenate(tiles, axis=1)).reshape(NPROJ, P, KT * P)
    out["w_out"] = items(get("w_out")[0]).reshape(KT, P, KT * P)
    w1, w2 = np.zeros((2, P, CMP_LEN, P), np.float32), np.zeros((P, 2, P), np.float32)
    pe = np.zeros((2, P, CMP_LEN), np.float32)
    for n, c in enumerate("kv"):
        for k in range(HKV):
            s = slice(k * DH, k * DH + DH)
            w1[n, s, :, s] = get(f"w_cmp{c}_1")[0].reshape(CMP_LEN, DH, DH).transpose(1, 0, 2)
            w2[s, n, s] = get(f"w_cmp{c}_2")[0]
            pe[n, s] = get(f"pe_cmp{c}")[0].T
    out["w1"], out["w2"], out["pe"] = w1, w2, pe
    out["pages"] = get("page_table").reshape(1, NPAGE)
    fkv = get("cache_fox_kv")[0]
    out["fox_k"] = fkv[:, :, 0].reshape(N_POOL, PAGE, 4, P).transpose(0, 3, 2, 1)
    out["fox_v"] = fkv[:, :, 1].reshape(N_POOL, PAGE, HF * DH)
    out["fox_lf"] = get("cache_fox_logf")[0].transpose(0, 2, 1)
    nkv = get("cache_nsa_kv")[0].reshape(N_POOL, PAGE, 4, P)
    out["nsa_t"] = nkv[:, :, 0:3].transpose(0, 3, 2, 1)
    out["nsa_v"] = nkv[:, :, 3]
    state = get("state_nsa_win_kv")[0].reshape(DEC, PAST, 2, P)
    out["win_k"] = state[:, :, 0].transpose(2, 0, 1)
    out["win_v"] = state[:, :, 1].reshape(NPAGE, PAGE, P).transpose(1, 0, 2)
    out["win_old"] = state.reshape(DEC * PAST, 2 * P)
    return {n: np.ascontiguousarray(a) for n, a in out.items()}


OUTPUTS = {"y": (P, KT, TOK), "fox": (8, P, TOK), "logf": (HF, TOK), "nsa": (4, P, TOK), "win": (2, P, TOK),
           "win_old": (DEC * PAST, 2 * P)}


def kernel(**inputs):
    import concourse.bacc as bacc
    from concourse.bass_utils import run_bass_kernel_spmd

    nc = bacc.Bacc("TRN2", target_bir_lowering=False, num_devices=1)
    arrays = lay_out(inputs)
    I = {n: nc.dram_tensor(f"in_{n}", a.shape, mybir.dt.from_np(a.dtype), kind="ExternalInput").ap()
         for n, a in arrays.items()}
    O = {n: nc.dram_tensor(f"out_{n}", s, F32, kind="ExternalOutput").ap() for n, s in OUTPUTS.items()}
    layer_kernel(nc, I, O)
    res = run_bass_kernel_spmd(nc, [{f"in_{n}": a for n, a in arrays.items()}], core_ids=[0]).results[0]
    got = {n: np.asarray(res[f"out_{n}"]) for n in OUTPUTS}

    y = got["y"].transpose(2, 1, 0).reshape(TOK, D_MODEL)
    fox = got["fox"].reshape(2, HF, DH, TOK).transpose(3, 0, 1, 2)
    logf = got["logf"].T
    nsa = got["nsa"].reshape(4, HKV, DH, TOK).transpose(3, 0, 1, 2)
    win = got["win"].reshape(2, HKV, DH, TOK).transpose(3, 0, 1, 2)
    old = got["win_old"].reshape(DEC, PAST, 2, HKV, DH)
    win_s = np.concatenate([old, win[SEQ:, None]], axis=1)

    def prompt(a):
        return np.ascontiguousarray(a[None, None, :SEQ])

    def sample(a):
        return np.ascontiguousarray(a[None, SEQ:, None])

    return (np.ascontiguousarray(y[None, :SEQ]), np.ascontiguousarray(y[SEQ:, None]),
            prompt(fox), prompt(logf), prompt(nsa), prompt(win),
            sample(fox), sample(logf), sample(nsa), np.ascontiguousarray(win_s[None]))
```
